# Optimizing a Trainium2 kernel written in Bass

```python
import math
import jax, jax.numpy as jnp
from jax import lax
import numpy as np

D_MODEL = 2048
BATCH = 1
SEQ = 256
DEPTH = 1

DIFF_HEADS = 8
DIFF_D = 64
NSA_HEADS = 8
NSA_KV = 2
NSA_GROUP = NSA_HEADS // NSA_KV
NSA_DK = 128
NSA_DV = 128
CMP_LEN = 32
CMP_STRIDE = 16
CMP_HIDDEN = 256
SLC_LEN = 64
SLC_TOPK = 16
WINDOW = 512
N_BUCKETS = 32
MAX_DISTANCE = 128
D_FF = 5632
CONV_W = 3
Q_BLOCK = 128
EPS = 1e-6
NEG = -1e30
FORCE = 1e30
TINY = 1e-30

DIFF_QK = DIFF_HEADS * 2 * DIFF_D
DIFF_V = DIFF_HEADS * 2 * DIFF_D
NSA_Q = NSA_HEADS * NSA_DK
NSA_K = NSA_KV * NSA_DK
NSA_V = NSA_KV * NSA_DV
N_GATES = NSA_HEADS * 3
SPLIT_SIZES = (DIFF_QK, DIFF_QK, DIFF_V, NSA_Q, NSA_K, NSA_V, NSA_K, NSA_V, NSA_K, NSA_V, N_GATES)
IN_COLS = 2 * DIFF_QK + DIFF_V + NSA_Q + 3 * (NSA_K + NSA_V) + N_GATES
MIX_WIDTH = DIFF_HEADS * 2 * DIFF_D + NSA_HEADS * NSA_DV


def rms_norm(x, g):
    xf = x.astype(jnp.float32)
    y = xf * lax.rsqrt(jnp.mean(xf * xf, axis=-1, keepdims=True) + EPS)
    return (y * g.astype(jnp.float32)).astype(x.dtype)

def rel_bucket(delta):
    n = jnp.maximum(delta, 0)
    max_exact = N_BUCKETS // 2
    nf = jnp.maximum(n, 1).astype(jnp.float32)
    large = max_exact + (jnp.log(nf / max_exact) / math.log(MAX_DISTANCE / max_exact)
                         * (N_BUCKETS - max_exact)).astype(jnp.int32)
    large = jnp.minimum(large, N_BUCKETS - 1)
    return jnp.where(n < max_exact, n, large)

def masked_softmax(s, mask):
    s = jnp.where(mask, s, NEG)
    m = jnp.max(s, axis=-1, keepdims=True)
    p = jnp.exp(s - m) * mask
    return p / jnp.maximum(jnp.sum(p, axis=-1, keepdims=True), TINY)

def selection_map(nb, nc):
    r = SLC_LEN // CMP_STRIDE
    j = np.arange(nb)[:, None, None]
    m = np.arange(r)[None, :, None]
    n = np.arange(CMP_LEN // CMP_STRIDE)[None, None, :]
    c = r * j - m - n
    jj = np.broadcast_to(j, c.shape)
    valid = (c >= 0) & (c < nc)
    out = np.zeros((nb, nc), np.float32)
    np.add.at(out, (jj[valid], c[valid]), 1.0)
    return out

def compress(k, pos_emb, w1, w2):
    B, S, G, d = k.shape
    nc = (S - CMP_LEN) // CMP_STRIDE + 1
    idx = jnp.arange(nc)[:, None] * CMP_STRIDE + jnp.arange(CMP_LEN)[None, :]
    blocks = k[:, idx] + pos_emb[:, None, :]
    blocks = jnp.transpose(blocks, (0, 3, 1, 2, 4)).reshape(B, G, nc, CMP_LEN * d)
    return jax.nn.gelu(blocks @ w1, approximate=True) @ w2

def diff_attention(q, k, v, lam, lam_init, subln, bias_tab):
    B, H, S, _, d = q.shape
    nblk = S // Q_BLOCK
    kpos = jnp.arange(S)
    scale = d ** -0.5

    def block(i):
        s0 = i * Q_BLOCK
        qb = lax.dynamic_slice_in_dim(q, s0, Q_BLOCK, axis=2)
        qpos = s0 + jnp.arange(Q_BLOCK)
        delta = qpos[:, None] - kpos[None, :]
        bias = jnp.transpose(bias_tab[rel_bucket(delta)], (2, 0, 1))
        logits = jnp.einsum('bhqmd,bhkmd->bhmqk', qb, k).astype(jnp.float32) * scale + bias[None, :, None]
        p = masked_softmax(logits, (delta >= 0)[None, None, None])
        a = p[:, :, 0] - lam * p[:, :, 1]
        return jnp.einsum('bhqk,bhke->bhqe', a.astype(v.dtype), v)

    o = lax.map(block, jnp.arange(nblk))
    o = jnp.transpose(o, (1, 2, 0, 3, 4)).reshape(B, H, S, 2 * d)
    return rms_norm(o, subln) * (1.0 - lam_init)

def nsa_attention(q, k_cmp, v_cmp, k_slc, v_slc, k_win, v_win, gates, bias_nsa):
    B, G, Hg, S, dk = q.shape
    nc = k_cmp.shape[2]
    nb = S // SLC_LEN
    topk = min(SLC_TOPK, nb)
    nsel = topk * SLC_LEN
    scale = dk ** -0.5
    sel_map = jnp.asarray(selection_map(nb, nc))
    cmp_end = jnp.arange(nc) * CMP_STRIDE + (CMP_LEN - 1)
    ks_blk = k_slc.reshape(B, G, nb, SLC_LEN, dk)
    vs_blk = v_slc.reshape(B, G, nb, SLC_LEN, -1)
    pad = ((0, 0), (0, 0), (WINDOW, 0), (0, 0))
    kw_pad = jnp.pad(k_win, pad)
    vw_pad = jnp.pad(v_win, pad)
    table_g = jnp.transpose(bias_nsa, (1, 0, 2))
    bi = jnp.arange(B)[:, None, None, None]
    gi = jnp.arange(G)[None, :, None, None]
    blk = jnp.arange(nb)

    def block(i):
        s0 = i * Q_BLOCK
        qb = lax.dynamic_slice_in_dim(q, s0, Q_BLOCK, axis=3)
        gb = lax.dynamic_slice_in_dim(gates, s0, Q_BLOCK, axis=3)
        qpos = s0 + jnp.arange(Q_BLOCK)
        lc = jnp.einsum('bghqd,bgcd->bghqc', qb, k_cmp).astype(jnp.float32) * scale
        pc = masked_softmax(lc, cmp_end[None, :] <= qpos[:, None])
        o_cmp = jnp.einsum('bghqc,bgcd->bghqd', pc.astype(v_cmp.dtype), v_cmp)
        imp = jnp.einsum('bgqc,jc->bgqj', jnp.sum(pc, axis=2), sel_map)
        cur = (qpos // SLC_LEN)[:, None]
        forced = (blk[None] == 0) | (blk[None] == cur) | (blk[None] == cur - 1)
        imp = jnp.where(forced, FORCE, jnp.where(blk[None] <= cur, imp, NEG))
        _, idx = lax.top_k(imp, topk)
        k_sel = ks_blk[bi, gi, idx].reshape(B, G, Q_BLOCK, nsel, dk)
        v_sel = vs_blk[bi, gi, idx].reshape(B, G, Q_BLOCK, nsel, -1)
        kpos_sel = (idx[..., None] * SLC_LEN + jnp.arange(SLC_LEN)).reshape(B, G, Q_BLOCK, nsel)
        d_sel = qpos[:, None] - kpos_sel
        b_sel = jnp.transpose(table_g[gi, rel_bucket(d_sel)], (0, 1, 4, 2, 3))
        ls = jnp.einsum('bghqd,bgqkd->bghqk', qb, k_sel).astype(jnp.float32) * scale + b_sel
        ps = masked_softmax(ls, (d_sel >= 0)[:, :, None])
        o_slc = jnp.einsum('bghqk,bgqkd->bghqd', ps.astype(v_sel.dtype), v_sel)
        kwb = lax.dynamic_slice_in_dim(kw_pad, s0, Q_BLOCK + WINDOW, axis=2)
        vwb = lax.dynamic_slice_in_dim(vw_pad, s0, Q_BLOCK + WINDOW, axis=2)
        kpos_w = s0 - WINDOW + jnp.arange(Q_BLOCK + WINDOW)
        d_w = qpos[:, None] - kpos_w[None, :]
        wmask = (d_w >= 0) & (d_w < WINDOW) & (kpos_w[None, :] >= 0)
        b_w = jnp.transpose(bias_nsa[rel_bucket(d_w)], (2, 3, 0, 1))
        lw = jnp.einsum('bghqd,bgkd->bghqk', qb, kwb).astype(jnp.float32) * scale + b_w
        pw = masked_softmax(lw, wmask)
        o_win = jnp.einsum('bghqk,bgkd->bghqd', pw.astype(vwb.dtype), vwb)
        return gb[..., 0:1] * o_cmp + gb[..., 1:2] * o_slc + gb[..., 2:3] * o_win

    o = lax.map(block, jnp.arange(S // Q_BLOCK))
    return jnp.transpose(o, (1, 2, 3, 0, 4, 5)).reshape(B, G, Hg, S, -1)

def causal_dwconv(u, w, b):
    S = u.shape[1]
    up = jnp.pad(u, ((0, 0), (CONV_W - 1, 0), (0, 0)))
    y = b
    for j in range(CONV_W):
        y = y + w[j] * up[:, j:j + S]
    return y

def first_inputs(seed: int = 0) -> dict:
    key = jax.random.key(seed)
    ks = jax.random.split(key, 24)
    f32 = jnp.float32

    def nrm(k, shape, scale):
        return jax.random.normal(k, shape, f32) * scale

    def gain(k, shape):
        return 1.0 + 0.05 * jax.random.normal(k, shape, f32)

    return {
        'x': nrm(ks[0], (BATCH, SEQ, D_MODEL), 1.0),
        'pre_mix_norm': gain(ks[1], (DEPTH, D_MODEL)),
        'w_in': nrm(ks[2], (DEPTH, D_MODEL, IN_COLS), D_MODEL ** -0.5),
        'lambda_q1': nrm(ks[3], (DEPTH, DIFF_D), 0.1),
        'lambda_k1': nrm(ks[4], (DEPTH, DIFF_D), 0.1),
        'lambda_q2': nrm(ks[5], (DEPTH, DIFF_D), 0.1),
        'lambda_k2': nrm(ks[6], (DEPTH, DIFF_D), 0.1),
        'diff_subln': gain(ks[7], (DEPTH, 2 * DIFF_D)),
        'cmp_pos_k': nrm(ks[8], (DEPTH, CMP_LEN, NSA_DK), 0.1),
        'cmp_pos_v': nrm(ks[9], (DEPTH, CMP_LEN, NSA_DV), 0.1),
        'cmp_k_w1': nrm(ks[10], (DEPTH, CMP_LEN * NSA_DK, CMP_HIDDEN), (CMP_LEN * NSA_DK) ** -0.5),
        'cmp_k_w2': nrm(ks[11], (DEPTH, CMP_HIDDEN, NSA_DK), CMP_HIDDEN ** -0.5),
        'cmp_v_w1': nrm(ks[12], (DEPTH, CMP_LEN * NSA_DV, CMP_HIDDEN), (CMP_LEN * NSA_DV) ** -0.5),
        'cmp_v_w2': nrm(ks[13], (DEPTH, CMP_HIDDEN, NSA_DV), CMP_HIDDEN ** -0.5),
        'rel_bias': nrm(ks[14], (N_BUCKETS, DIFF_HEADS + NSA_HEADS), 0.5),
        'w_out': nrm(ks[15], (DEPTH, MIX_WIDTH, D_MODEL), MIX_WIDTH ** -0.5),
        'post_mix_norm': gain(ks[16], (DEPTH, D_MODEL)),
        'pre_ffn_norm': gain(ks[17], (DEPTH, D_MODEL)),
        'w_up': nrm(ks[18], (DEPTH, D_MODEL, 2 * D_FF), D_MODEL ** -0.5),
        'conv_w': nrm(ks[19], (DEPTH, CONV_W, 2 * D_FF), CONV_W ** -0.5),
        'conv_b': nrm(ks[20], (DEPTH, 2 * D_FF), 0.01),
        'w_down': nrm(ks[21], (DEPTH, D_FF, D_MODEL), D_FF ** -0.5),
        'post_ffn_norm': gain(ks[22], (DEPTH, D_MODEL)),
    }

def first_block(x, pre_mix_norm, w_in, lambda_q1, lambda_k1, lambda_q2, lambda_k2, diff_subln,
              cmp_pos_k, cmp_pos_v, cmp_k_w1, cmp_k_w2, cmp_v_w1, cmp_v_w2, rel_bias, w_out,
              post_mix_norm, pre_ffn_norm, w_up, conv_w, conv_b, w_down, post_ffn_norm):
    B, S, _ = x.shape
    f32 = jnp.float32
    offsets = np.cumsum(SPLIT_SIZES)[:-1].tolist()
    bias_diff = rel_bias[:, :DIFF_HEADS]
    bias_nsa = rel_bias[:, DIFF_HEADS:].reshape(N_BUCKETS, NSA_KV, NSA_GROUP)
    for l in range(DEPTH):
        h = rms_norm(x, pre_mix_norm[l])
        proj = h @ w_in[l]
        (dq, dk, dv, nq, kc, vc, ksl, vsl, kwn, vwn, g) = jnp.split(proj, offsets, axis=-1)
        q_d = dq.reshape(B, S, DIFF_HEADS, 2, DIFF_D).transpose(0, 2, 1, 3, 4)
        k_d = dk.reshape(B, S, DIFF_HEADS, 2, DIFF_D).transpose(0, 2, 1, 3, 4)
        v_d = dv.reshape(B, S, DIFF_HEADS, 2 * DIFF_D).transpose(0, 2, 1, 3)
        lam_init = 0.8 - 0.6 * math.exp(-0.3 * l)
        lam = (jnp.exp(jnp.sum(lambda_q1[l].astype(f32) * lambda_k1[l].astype(f32)))
               - jnp.exp(jnp.sum(lambda_q2[l].astype(f32) * lambda_k2[l].astype(f32))) + lam_init)
        o_diff = diff_attention(q_d, k_d, v_d, lam, lam_init, diff_subln[l], bias_diff)
        q_n = nq.reshape(B, S, NSA_KV, NSA_GROUP, NSA_DK).transpose(0, 2, 3, 1, 4)
        k_c = compress(kc.reshape(B, S, NSA_KV, NSA_DK), cmp_pos_k[l], cmp_k_w1[l], cmp_k_w2[l])
        v_c = compress(vc.reshape(B, S, NSA_KV, NSA_DV), cmp_pos_v[l], cmp_v_w1[l], cmp_v_w2[l])
        k_s = ksl.reshape(B, S, NSA_KV, NSA_DK).transpose(0, 2, 1, 3)
        v_s = vsl.reshape(B, S, NSA_KV, NSA_DV).transpose(0, 2, 1, 3)
        k_w = kwn.reshape(B, S, NSA_KV, NSA_DK).transpose(0, 2, 1, 3)
        v_w = vwn.reshape(B, S, NSA_KV, NSA_DV).transpose(0, 2, 1, 3)
        gates = jax.nn.sigmoid(g.reshape(B, S, NSA_KV, NSA_GROUP, 3)).transpose(0, 2, 3, 1, 4)
        o_nsa = nsa_attention(q_n, k_c, v_c, k_s, v_s, k_w, v_w, gates, bias_nsa)
        mix = jnp.concatenate([o_diff.transpose(0, 2, 1, 3).reshape(B, S, -1),
                               o_nsa.transpose(0, 3, 1, 2, 4).reshape(B, S, -1)], axis=-1)
        x = x + rms_norm(mix @ w_out[l], post_mix_norm[l])
        h = rms_norm(x, pre_ffn_norm[l])
        u = causal_dwconv(h @ w_up[l], conv_w[l], conv_b[l])
        gate, up = jnp.split(u, 2, axis=-1)
        y = (jax.nn.gelu(gate, approximate=True) * up) @ w_down[l]
        x = x + rms_norm(y, post_ffn_norm[l])
    return x


N_MIXERS = 2
N_A_LAYERS = (DEPTH + N_MIXERS - 1) // N_MIXERS
N_B_LAYERS = DEPTH // N_MIXERS
HGRN_EXPAND = 128
HGRN_HEADS = D_MODEL // HGRN_EXPAND
HGRN_KEY_DIM = HGRN_HEADS * HGRN_EXPAND
HGRN_HEAD_V = D_MODEL // HGRN_HEADS
CHUNK = 64
CONV_WIDTH = 3
FFN_DIM = 5632


def rmsnorm(x, w):
    x32 = x.astype(jnp.float32)
    y = x32 * lax.rsqrt(jnp.mean(x32 * x32, axis=-1, keepdims=True) + EPS)
    return (y * w.astype(jnp.float32)).astype(x.dtype)

def dwconv3(z, w):
    L = z.shape[1]
    zp = jnp.pad(z, ((0, 0), (1, 1), (0, 0)))
    return w[0] * zp[:, :L] + w[1] * zp[:, 1:L + 1] + w[2] * zp[:, 2:]

def chunked_gated_recurrence(q, k, log_f, v):
    N, H, L, K = q.shape
    V = v.shape[-1]
    n_chunks = L // CHUNK

    def to_chunks(t):
        return t.reshape(N, H, n_chunks, CHUNK, t.shape[-1]).transpose(2, 0, 1, 3, 4)

    causal_in_chunk = jnp.tril(jnp.ones((CHUNK, CHUNK), dtype=bool))[:, :, None]

    def step(S, inp):
        qi, ki, gi, vi = inp
        b = jnp.cumsum(gi, axis=2)
        inter = jnp.einsum('nhtk,nhkv->nhtv', qi * jnp.exp(b), S)
        diff = b[:, :, :, None, :] - b[:, :, None, :, :]
        decay = jnp.exp(jnp.where(causal_in_chunk, diff, -jnp.inf))
        scores = jnp.einsum('nhtk,nhsk,nhtsk->nhts', qi, ki, decay)
        intra = jnp.einsum('nhts,nhsv->nhtv', scores, vi)
        b_last = b[:, :, -1]
        k_dec = ki * jnp.exp(b_last[:, :, None, :] - b)
        S_new = jnp.exp(b_last)[..., None] * S + jnp.einsum('nhck,nhcv->nhkv', k_dec, vi)
        return S_new, inter + intra

    S0 = jnp.zeros((N, H, K, V), jnp.float32)
    _, o = lax.scan(step, S0, (to_chunks(q), to_chunks(k), to_chunks(log_f), to_chunks(v)))
    return o.transpose(1, 2, 0, 3, 4).reshape(N, H, L, V)

def hgrn2_mixer(h, w_in, w_out, g_norm_w, lb_fwd, lb_bwd):
    B_, L, _ = h.shape
    K, D = HGRN_KEY_DIM, D_MODEL
    u = h @ w_in
    q, f_f, f_b, v, g = jnp.split(u, [K, 2 * K, 3 * K, 3 * K + D], axis=-1)
    q = jax.nn.silu(q)

    def gates(f_raw, lb):
        f = lb + (1.0 - lb) * jax.nn.sigmoid(f_raw.astype(jnp.float32))
        return 1.0 - f, jnp.log(f)

    k_f, lf_f = gates(f_f, lb_fwd)
    k_b, lf_b = gates(f_b, lb_bwd)

    def heads(t, d):
        return t.reshape(t.shape[0], L, HGRN_HEADS, d).transpose(0, 2, 1, 3).astype(jnp.float32)

    rev = lambda t: t[:, ::-1]
    qs = heads(jnp.concatenate([q, rev(q)], axis=0), HGRN_EXPAND)
    ks = heads(jnp.concatenate([k_f, rev(k_b)], axis=0), HGRN_EXPAND)
    ls = heads(jnp.concatenate([lf_f, rev(lf_b)], axis=0), HGRN_EXPAND)
    vs = heads(jnp.concatenate([v, rev(v)], axis=0), HGRN_HEAD_V)
    o = chunked_gated_recurrence(qs, ks, ls, vs)
    o = o[:B_] + o[B_:, :, ::-1]
    o = o.transpose(0, 2, 1, 3)
    gh = g.reshape(B_, L, HGRN_HEADS, HGRN_HEAD_V)
    o = rmsnorm(o, g_norm_w) * jax.nn.silu(gh.astype(jnp.float32))
    return o.reshape(B_, L, D).astype(h.dtype) @ w_out

def short_conv_mixer(h, w_in, w_conv, w_out):
    u = h @ w_in
    gate_b, gate_c, x_in = jnp.split(u, 3, axis=-1)
    z = dwconv3(gate_c * x_in, w_conv)
    return (gate_b * z) @ w_out

def conv_ffn(h, w_in, w_conv, w_out):
    up = dwconv3(h @ w_in, w_conv)
    gate, val = jnp.split(up, 2, axis=-1)
    return (jax.nn.silu(gate) * val) @ w_out

def second_inputs(seed: int = 0) -> dict:
    key = jax.random.key(seed)
    ks = jax.random.split(key, 16)
    D, K, F = D_MODEL, HGRN_KEY_DIM, FFN_DIM
    nrm = lambda k, shape, scale: jax.random.normal(k, shape, jnp.float32) * scale
    return {
        "x": nrm(ks[0], (BATCH, SEQ, D), 1.0),
        "hgrn_w_in": nrm(ks[1], (N_A_LAYERS, D, 3 * K + 2 * D), D ** -0.5),
        "hgrn_w_out": nrm(ks[2], (N_A_LAYERS, D, D), D ** -0.5),
        "hgrn_gnorm": 1.0 + nrm(ks[3], (N_A_LAYERS, HGRN_HEAD_V), 0.02),
        "hgrn_lower_bounds": nrm(ks[4], (2, N_A_LAYERS, K), 1.0),
        "sconv_w_in": nrm(ks[5], (N_B_LAYERS, D, 3 * D), D ** -0.5),
        "sconv_w_conv": nrm(ks[6], (N_B_LAYERS, CONV_WIDTH, D), CONV_WIDTH ** -0.5),
        "sconv_w_out": nrm(ks[7], (N_B_LAYERS, D, D), D ** -0.5),
        "ffn_w_in": nrm(ks[8], (DEPTH, D, 2 * F), D ** -0.5),
        "ffn_w_conv": nrm(ks[9], (DEPTH, CONV_WIDTH, 2 * F), CONV_WIDTH ** -0.5),
        "ffn_w_out": nrm(ks[10], (DEPTH, F, D), F ** -0.5),
        "norm_pre_mix": 1.0 + nrm(ks[11], (DEPTH, D), 0.02),
        "norm_post_mix": 1.0 + nrm(ks[12], (DEPTH, D), 0.02),
        "norm_pre_ffn": 1.0 + nrm(ks[13], (DEPTH, D), 0.02),
        "norm_post_ffn": 1.0 + nrm(ks[14], (DEPTH, D), 0.02),
    }

def second_block(x, hgrn_w_in, hgrn_w_out, hgrn_gnorm, hgrn_lower_bounds,
              sconv_w_in, sconv_w_conv, sconv_w_out,
              ffn_w_in, ffn_w_conv, ffn_w_out,
              norm_pre_mix, norm_post_mix, norm_pre_ffn, norm_post_ffn):
    lb = jnp.cumsum(jax.nn.softmax(hgrn_lower_bounds.astype(jnp.float32), axis=1), axis=1)
    lb = lb - lb[:, :1]
    for i in range(DEPTH):
        j = i // N_MIXERS
        h = rmsnorm(x, norm_pre_mix[i])
        if i % N_MIXERS == 0:
            m = hgrn2_mixer(h, hgrn_w_in[j], hgrn_w_out[j], hgrn_gnorm[j], lb[0, j], lb[1, j])
        else:
            m = short_conv_mixer(h, sconv_w_in[j], sconv_w_conv[j], sconv_w_out[j])
        x = x + rmsnorm(m, norm_post_mix[i])
        h = rmsnorm(x, norm_pre_ffn[i])
        x = x + rmsnorm(conv_ffn(h, ffn_w_in[i], ffn_w_conv[i], ffn_w_out[i]), norm_post_ffn[i])
    return x


def setup_inputs(seed=0):
    out = dict(first_inputs(seed))
    for name, value in second_inputs(seed + 1).items():
        if name != "x":
            out[name + "_2"] = value
    return out


def reference(
    x, pre_mix_norm, w_in, lambda_q1, lambda_k1, lambda_q2, lambda_k2, diff_subln, cmp_pos_k,
    cmp_pos_v, cmp_k_w1, cmp_k_w2, cmp_v_w1, cmp_v_w2, rel_bias, w_out, post_mix_norm,
    pre_ffn_norm, w_up, conv_w, conv_b, w_down, post_ffn_norm, hgrn_w_in_2, hgrn_w_out_2,
    hgrn_gnorm_2, hgrn_lower_bounds_2, sconv_w_in_2, sconv_w_conv_2, sconv_w_out_2, ffn_w_in_2,
    ffn_w_conv_2, ffn_w_out_2, norm_pre_mix_2, norm_post_mix_2, norm_pre_ffn_2, norm_post_ffn_2,
):
    x = first_block(
        x, pre_mix_norm, w_in, lambda_q1, lambda_k1, lambda_q2, lambda_k2, diff_subln,
        cmp_pos_k, cmp_pos_v, cmp_k_w1, cmp_k_w2, cmp_v_w1, cmp_v_w2, rel_bias, w_out,
        post_mix_norm, pre_ffn_norm, w_up, conv_w, conv_b, w_down, post_ffn_norm,
    )
    return second_block(
        x, hgrn_w_in_2, hgrn_w_out_2, hgrn_gnorm_2, hgrn_lower_bounds_2, sconv_w_in_2,
        sconv_w_conv_2, sconv_w_out_2, ffn_w_in_2, ffn_w_conv_2, ffn_w_out_2, norm_pre_mix_2,
        norm_post_mix_2, norm_pre_ffn_2, norm_post_ffn_2,
    )


_drawn_inputs = setup_inputs


def setup_inputs(seed=0):
    import zlib

    import numpy as np

    out = dict(_drawn_inputs(seed))
    spreads = {}
    factors = {'lambda_q2': 51.384,
     'cmp_pos_k': 8.0,
     'conv_b': 5.499,
     'hgrn_gnorm_2': 16.437,
     'norm_pre_mix_2': 3.585,
     'norm_post_mix_2': 4.931,
     'norm_pre_ffn_2': 4.331,
     'norm_post_ffn_2': 23.139}
    for name, (base, spread) in spreads.items():
        noise = np.random.default_rng([zlib.crc32(name.encode()), seed]).standard_normal(out[name].shape)
        drawn = base * np.exp(spread * noise) if base else spread * noise
        out[name] = __import__('jax').numpy.asarray(drawn.astype(out[name].dtype))
    for name, factor in factors.items():
        out[name] = (out[name] * factor).astype(out[name].dtype)
    return out
```

```python
import math
from contextlib import ExitStack

import concourse.bass as bass
from concourse import mybir

ALU = mybir.AluOpType
ACT = mybir.ActivationFunctionType
F32 = mybir.dt.float32
F32R = mybir.dt.float32r
U8 = mybir.dt.uint8
AX = mybir.AxisListType

P = 128
S = 256
NT = S // P
D = 2048
KT = D // P
GC = 512
CK = 2
RING = 4
CPG = KT // CK
F = 5632
FT = F // P
DCH = FT // CK
NG = D // GC
FG = F // GC
EPS = 1e-6
NEG = -1e30
TINY = 1e-30

DIFF_H, NSA_H, NSA_KV = 8, 8, 2
NSA_GROUP = NSA_H // NSA_KV
DV, KC, VC, KS, VS, KW, VW = 2048, 4096, 4352, 4608, 4864, 5120, 5376
G0 = 5632
NGATE = 24
IN1 = G0 // GC
CMP_L, CMP_STRIDE, HID = 32, 16, 256
NC_ = (S - CMP_L) // CMP_STRIDE + 1
NCG = NSA_KV * NC_
CMP_LPC = CK * GC // HID
CMP_CH = CMP_L // CMP_LPC
LAM_INIT = 0.8 - 0.6 * math.exp(-0.3 * 0)
TOEP = 3 * P - 1
N_BUCKETS = 32

HPG = GC // P
HJ = D // GC
HGRP = 5
HCH = HGRP * CPG
N_LEV = 8
N_STEP = N_LEV + 1

TURN = ([KC, KC + P, VC, VC + P] + [P * j for j in range(16)] + [3072 + P * j for j in range(8)]
        + [KS, KS + P, KW, KW + P])
T_KC, T_VC, T_DQ, T_DK, T_NQ, T_KS, T_KW = 0, 2, 4, 12, 20, 28, 30


def bass_two_blocks(nc, T):
    with ExitStack() as ctx:
        def sb(name, shape, dt=F32, where=ctx):
            return where.enter_context(nc.sbuf_tensor(name, shape, dt))

        made = {}

        def sem(name):
            if name not in made:
                made[name] = ctx.enter_context(nc.semaphore(name))
            return made[name]

        raw = sb("raw", [P, RING, CK * GC])
        whi = sb("whi", [P, RING, CK * GC], F32R)
        wlo = sb("wlo", [P, RING, CK * GC], F32R)
        x = sb("x", [P, NT, D])
        ident = sb("ident", [P, P])
        gains = sb("gains", [P, 4, KT])
        taps = sb("taps", [P, 2, 4, 2 * FT])
        rstd = sb("rstd", [P, 4, NT])
        prs = sb("prs", [P, 4, NT])
        prime = sb("prime", [P, 1])
        psq = sb("psq", [P, 4, NT, NG])

        with ExitStack() as r:
            ybuf = sb("ybuf", [P, NT, D], where=r)
            hhi = sb("hhi", [P, FT, S], F32R, r)
            hlo = sb("hlo", [P, FT, S], F32R, r)
        with ExitStack() as r:
            utok = [sb(f"utok{j}", [P, NT, GC], where=r) for j in range(2)]
            cvg = sb("cvg", [P, 4, S], where=r)
            cvu = sb("cvu", [P, 4, S], where=r)
        with ExitStack() as r:
            sqj = sb("sqj", [P, D], where=r)
        with ExitStack() as r:
            ptok = sb("ptok", [P, NT, G0], where=r)
            qkT = sb("qkT", [P, 32, S], where=r)
            bias = sb("bias", [P, 16, S], where=r)
            wg = sb("wg", [P, KT, NGATE], where=r)
            wghi = sb("wghi", [P, KT, NGATE], F32R, r)
            wglo = sb("wglo", [P, KT, NGATE], F32R, r)
            gate = sb("gate", [P, NT, NGATE], where=r)
            posT = sb("posT", [P, 2, CMP_L], where=r)
            w2 = sb("w2", [P, 2, 2, P], where=r)
            hidT = sb("hidT", [P, 2, 2, NCG], where=r)
            kcmpT = sb("kcmpT", [P, NCG], where=r)
            vcmp = sb("vcmp", [NC_, NSA_KV, P], where=r)
            cmask = sb("cmask", [P, 2, NT, NC_], where=r)
            sub = sb("sub", [P, P], where=r)
            lam4 = sb("lam4", [P, 4, 64], where=r)
            lamv = sb("lamv", [P, 8], where=r)
            pc = sb("pc", [P, NT, NSA_H, NC_], where=r)
            pcs = sb("pcs", [P, 4, NT, NSA_H], where=r)
            nmx = sb("nmx", [P, 32, 2], where=r)
            psm = sb("psm", [P, 32, 2], where=r)
            cof = sb("cof", [P, 32, 2], where=r)
            dsq = sb("dsq", [P, NT, DIFF_H], where=r)
            drs = sb("drs", [P, NT, DIFF_H], where=r)
        mix1 = ptok
        with ExitStack() as r:
            sb("hold0", [P, NT, G0], where=r)
            pst = sb("pst", [P, 8, P], where=r)
            tabaug = sb("tabaug", [N_BUCKETS + 1, 16], where=r)
            onehot = sb("onehot", [N_BUCKETS + 1, TOEP], where=r)
            toep = sb("toep", [16, TOEP], where=r)
        with ExitStack() as r:
            sb("hold1", [P, NT, G0], where=r)
            gbo1 = sb("gbo1", [P, D], where=r)
        with ExitStack() as r:
            mix2 = sb("mix2", [P, NT, D], where=r)
            gbo2 = sb("gbo2", [P, D], where=r)
            stg = sb("stg", [P, 3, NT, GC], where=r)
            sgm = sb("sgm", [P, NT, GC], where=r)
            qT = sb("qT", [P, HPG, S], where=r)
            kf = sb("kf", [P, HPG, S], where=r)
            kb = sb("kb", [P, HPG, S], where=r)
            pf = sb("pf", [P, HPG, S], where=r)
            sf = sb("sf", [P, HPG, S], where=r)
            ib = sb("ib", [P, HPG, S], where=r)
            eb = sb("eb", [P, HPG, S], where=r)
            qd = [sb(f"qd{j}", [P, HPG, S], where=r) for j in range(2)]
            kd = [sb(f"kd{j}", [P, HPG, S], where=r) for j in range(2)]
            at = sb("at", [P, HPG, NT, S], where=r)
            ad = sb("ad", [P, HPG, NT, 32], where=r)
            vt = sb("vt", [P, NT, GC], where=r)
            gs = sb("gs", [P, NT, GC], where=r)
            hsq = sb("hsq", [P, NT, 16], where=r)
            hrs = sb("hrs", [P, NT, 16], where=r)
            lmask = sb("lmask", [P, 6, 32], where=r)
            lpick = sb("lpick", [P, HPG * NT, 32], where=r)
            gnb = sb("gnb", [P, P], where=r)
        sb("hold2", [P, NT * D + 2 * FT * S + 512])
        with ExitStack() as r:
            ahi = sb("ahi", [P, KT, S], F32R, r)
            alo = sb("alo", [P, KT, S], F32R, r)
        with ExitStack() as r:
            blk = sb("blk", [P, 2, CMP_L, NCG], where=r)
        with ExitStack() as r:
            scb = [sb(f"scb{j}", [P, 2, S], where=r) for j in range(2)]
            prb = [sb(f"prb{j}", [P, 2, S], where=r) for j in range(2)]
            pts = [sb(f"pts{j}", [P, 5 * P], where=r) for j in range(2)]
            blkhi = sb("blkhi", [P, 2, CMP_L, NCG], F32R, r)
            blklo = sb("blklo", [P, 2, CMP_L, NCG], F32R, r)
        with ExitStack() as r:
            gbd = sb("gbd", [P, D], where=r)

        acc = [ctx.enter_context(nc.psum_tensor(f"acc{i}", [P, NT, GC], F32)) for i in range(2)]
        tp = [ctx.enter_context(nc.psum_tensor(f"tp{i}", [P, 4, S], F32)) for i in range(2)]

        landed = [sem(f"landed{i}") for i in range(RING)]
        hi_done, lo_done, chunk_used = sem("hi_done"), sem("lo_done"), sem("chunk_used")
        group_free = sem("group_free")

        cb, gb = {}, {}
        n = g = 0
        for name, chunks, groups in (("in1", IN1 * CPG, IN1), ("cmp", 2 * CMP_CH, 0), ("out1", NG * CPG, NG),
                                     ("up1", 2 * FG * CPG, 2 * FG), ("down1", NG * DCH, NG),
                                     ("in2", HJ * HCH, HJ * HGRP), ("out2", NG * CPG, NG),
                                     ("up2", 2 * FG * CPG, 2 * FG), ("down2", NG * DCH, NG)):
            cb[name], gb[name] = n, g
            assert n % RING == 0
            n += chunks
            g += groups

        def load(sp, n, s, src, kk=CK):
            dst = raw[:, s, :].rearrange("p (k c) -> p k c", k=kk)
            if not (isinstance(n, int) and n < RING):
                sp.wait_ge(lo_done, n - RING + 1)
            sp.dma_start(dst, src).then_inc(landed[s], 16)

        def split_hi(act, n, s, turn):
            act.wait_ge(landed[s], turn)
            if not (isinstance(n, int) and n < RING):
                act.wait_ge(chunk_used, n - RING + 1)
            act.activation(whi[:, s, :], raw[:, s, :], ACT.Copy).then_inc(hi_done, 1)

        def split_lo(dve, n, s):
            dve.wait_ge(hi_done, n + 1)
            dve.tensor_tensor(wlo[:, s, :], raw[:, s, :], whi[:, s, :].bitcast(F32),
                              ALU.subtract).then_inc(lo_done, 1)

        def products(pe, n, s, out, xhi, xlo, k0, nk, ready=None):
            pe.wait_ge(lo_done, n + 1)
            for k in range(CK):
                kt = k0 + k
                if ready:
                    pe.wait_ge(sem("pre_lo"), lo_ready(ready, kt))
                c = slice(k * GC, (k + 1) * GC)
                for t in range(NT):
                    xh, xl = xhi[:, kt, t * P:(t + 1) * P], xlo[:, kt, t * P:(t + 1) * P]
                    pe.matmul(out[:, t, :], xh, whi[:, s, c], start=(kt == 0), stop=False)
                    pe.matmul(out[:, t, :], xh, wlo[:, s, c], start=False, stop=False)
                    mm = pe.matmul(out[:, t, :], xl, whi[:, s, c], start=False, stop=(kt == nk - 1))
            mm.then_inc(chunk_used, 1)

        def group(pe, g):
            if not (isinstance(g, int) and g < 2):
                pe.wait_ge(group_free, g - 1)

        def s_hi(act, ph, i, per, c):
            n = cb[ph] + c + i * per
            split_hi(act, n, c % RING, 16 * (cb[ph] // RING + c // RING + 1) + i * (16 * (per // RING)))

        def s_lo(dve, ph, i, per, c):
            split_lo(dve, cb[ph] + c + i * per, c % RING)

        def s_load(sp, ph, i, per, c, src, kk=CK):
            load(sp, cb[ph] + c + i * per, c % RING, src, kk)

        def w_tile(w, k0, col):
            return w[k0 * P:(k0 + CK) * P, bass.ds(col, GC)].rearrange("(k p) c -> p k c", p=P)

        PRE = ("in1", "out1", "up1", "in2", "out2", "up2")

        def lo_ready(ph, kt):
            return KT * PRE.index(ph) + kt + 1

        def pre_pe(pe, ph, src, ready):
            for q in range(4):
                ready(pe, q)
                if q >= 2:
                    pe.wait_ge(sem("pre_lo"), lo_ready(ph, 4 * q - 5))
                for k in range(4):
                    for t in range(NT):
                        c = (4 * q + k) * P
                        mm = pe.transpose(tp[q % 2][:, k, t * P:(t + 1) * P], src[:, t, c:c + P], ident[:, :])
                mm.then_inc(sem("pre_turned"), 1)

        def pre_act(act, ph, gain):
            for q in range(4):
                act.wait_ge(sem("pre_turned"), 4 * PRE.index(ph) + q + 1)
                for k in range(4):
                    kt = 4 * q + k
                    act.activation(ahi[:, kt, :], tp[q % 2][:, k, :], ACT.Copy,
                                   scale=1.0 if gain is None else gains[:, gain, kt:kt + 1])\
                       .then_inc(sem("pre_hi"), 1)

        def pre_dve(dve, ph, gain):
            for kt in range(KT):
                dve.wait_ge(sem("pre_hi"), lo_ready(ph, kt | 1))
                turned, hi = tp[kt // 4 % 2][:, kt % 4, :], ahi[:, kt, :].bitcast(F32)
                if gain is None:
                    i = dve.tensor_tensor(alo[:, kt, :], turned, hi, ALU.subtract)
                else:
                    i = dve.scalar_tensor_tensor(out=alo[:, kt, :], in0=turned, scalar=gains[:, gain, kt:kt + 1],
                                                 in1=hi, op0=ALU.mult, op1=ALU.subtract)
                i.then_inc(sem("pre_lo"), 1)

        def sumsq_act(act, ph, k, x_sem, x_count):
            act.wait_ge(x_sem, x_count)
            for t in range(NT):
                if t:
                    act.wait_ge(sem(f"{ph}_sq"), 1)
                act.activation(sqj[:, :], x[:, t, :], ACT.Square,
                               accum_out=rstd[:, k, t:t + 1]).then_inc(sem(f"{ph}_sq"), 1)
            act.wait_ge(sem(f"{ph}_ms"), 1)
            act.activation(rstd[:, k, :], rstd[:, k, :], ACT.Sqrt).then_inc(sem(f"{ph}_root"), 1)

        def sumsq_dve(dve, ph, k):
            dve.wait_ge(sem(f"{ph}_sq"), NT)
            dve.tensor_scalar(rstd[:, k, :], rstd[:, k, :], 1.0 / D, EPS, ALU.mult, ALU.add)\
               .then_inc(sem(f"{ph}_ms"), 1)
            dve.wait_ge(sem(f"{ph}_root"), 1)
            dve.reciprocal(rstd[:, k, :], rstd[:, k, :]).then_inc(sem(f"{ph}_rstd"), 1)

        def back_load(sp, ph, w, nch):
            with sp.Fori(0, 2) as i:
                for c in range(2 * nch):
                    s_load(sp, ph, i, 2 * nch, c, w_tile(w, CK * (c % nch), i * (2 * GC) + c // nch * GC))

        def back_pe(pe, ph, xhi, xlo, nch, ready, ready_count, last_count=None):
            pe.wait_ge(ready, ready_count)
            with pe.Fori(0, 2) as i:
                for c in range(2 * nch):
                    if c % nch == 0:
                        group(pe, gb[ph] + c // nch + 2 * i)
                    if last_count and CK * c == 4 * (FG - 1):
                        pe.wait_ge(ready, last_count)
                    products(pe, cb[ph] + c + i * (2 * nch), c % RING, acc[(gb[ph] + c // nch) % 2],
                             xhi, xlo, CK * (c % nch), CK * nch)

        def back_group_dve(dve, ph, i, gg, nch, gain_row):
            dve.wait_ge(sem(f"{ph}_gain"), 16)
            dve.wait_ge(chunk_used, cb[ph] + (gg + 1) * nch + i * (2 * nch))
            a = acc[(gb[ph] + gg) % 2]
            col = i * (2 * GC) + gg * GC
            for t in range(NT):
                dve.tensor_tensor(ybuf[:, t, bass.ds(col, GC)], a[:, t, :], gain_row[:, bass.ds(col, GC)],
                                  ALU.mult).then_inc(sem(f"{ph}_y"), 1)

        def back_group_act(act, ph, k, i, gg):
            act.wait_ge(sem(f"{ph}_y"), i * 4 + (2 * gg + 2))
            a = acc[(gb[ph] + gg) % 2]
            for t in range(NT):
                m = act.activation(a[:, t, :], a[:, t, :], ACT.Square,
                                   accum_out=psq[:, k, t, bass.ds(i * 2 + gg, 1)])
            m.then_inc(group_free, 1)

        def back_act(act, ph, k, nch):
            with act.Fori(0, 2) as i:
                for c in range(2 * nch):
                    s_hi(act, ph, i, 2 * nch, c)
                    if c == nch + 3:
                        back_group_act(act, ph, k, i, 0)
                back_group_act(act, ph, k, i, 1)
            act.wait_ge(sem(f"{ph}_pms"), 2)
            act.activation(prs[:, k, :], prs[:, k, :], ACT.Sqrt).then_inc(sem(f"{ph}_proot"), 1)

        def back_dve(dve, ph, k, nch, gain_row):
            with dve.Fori(0, 2) as i:
                for c in range(2 * nch):
                    s_lo(dve, ph, i, 2 * nch, c)
                    if c == nch + 3:
                        back_group_dve(dve, ph, i, 0, nch, gain_row)
                back_group_dve(dve, ph, i, 1, nch, gain_row)
            dve.wait_ge(group_free, gb[ph] + NG)
            dve.tensor_reduce(prs[:, k, :], psq[:, k, :, :], AX.X, ALU.add).then_inc(sem(f"{ph}_pms"), 1)
            dve.wait_ge(sem(f"{ph}_pms"), 1)
            dve.tensor_scalar(prs[:, k, :], prs[:, k, :], 1.0 / D, EPS, ALU.mult, ALU.add)\
               .then_inc(sem(f"{ph}_pms"), 1)
            dve.wait_ge(sem(f"{ph}_proot"), 1)
            dve.reciprocal(prs[:, k, :], prs[:, k, :]).then_inc(sem(f"{ph}_prs"), 1)
            dve.wait_ge(sem(f"{ph}_prs"), 1)
            for q in range(4):
                c = slice(q * GC, (q + 1) * GC)
                for t in range(NT):
                    dve.scalar_tensor_tensor(out=x[:, t, c], in0=ybuf[:, t, c], scalar=prs[:, k, t:t + 1],
                                             in1=x[:, t, c], op0=ALU.mult, op1=ALU.add)\
                       .then_inc(sem(f"{ph}_x"), 1)

        def x_ready(ph):
            def wait(e, q):
                e.wait_ge(sem(f"{ph}_x"), 2 * q + 2)
            return wait

        BODY = 2 * CPG

        def up_load(sp, ph, w):
            def body(i):
                for c in range(BODY):
                    s_load(sp, ph, i, BODY, c, w_tile(w, CK * (c % CPG), i * GC + c // CPG * F))
            with sp.Fori(0, FG) as i:
                body(i)

        def up_pe(pe, ph):
            def turn(i, half):
                pe.wait_ge(group_free, gb[ph] + half + 1 + i * 2)
                for k in range(4):
                    for t in range(NT):
                        mm = pe.transpose(tp[half][:, k, t * P:(t + 1) * P], utok[half][:, t, k * P:(k + 1) * P],
                                          ident[:, :])
                mm.then_inc(sem(f"{ph}_uturned{half}"), 1)

            def body(i, first):
                for c in range(BODY):
                    if c % CPG == 0:
                        group(pe, gb[ph] + c // CPG + i * 2)
                    products(pe, cb[ph] + c + i * BODY, c % RING, acc[(gb[ph] + c // CPG) % 2], ahi, alo,
                             CK * (c % CPG), KT, ph if first and c < CPG else None)
                    if c == 1 and not first:
                        turn(i - 1, 1)
                    if c == CPG + 1:
                        turn(i, 0)
            body(0, True)
            with pe.Fori(1, FG) as i:
                body(i, False)
            turn(FG - 1, 1)

        def up_act(act, ph, b, x_sem, x_count):
            cv = (cvg, cvu)

            def evacuate(i, half):
                act.wait_ge(chunk_used, cb[ph] + CPG * (half + 1) + i * BODY)
                for t in range(NT):
                    m = act.activation(utok[half][:, t, :], acc[(gb[ph] + half) % 2][:, t, :], ACT.Copy,
                                       scale=rstd[:, 2 * b + 1, t:t + 1])
                m.then_inc(group_free, 1)

            def centre(i, half):
                act.wait_ge(sem(f"{ph}_uturned{half}"), i + 1)
                act.wait_ge(sem(f"{ph}_hid"), i + 1)
                for k in range(4):
                    ct = i * 4 + (half * FT + k)
                    act.activation(cv[half][:, k, :], tp[half][:, k, :], ACT.Identity,
                                   bias=taps[:, b, 3, bass.ds(ct, 1)],
                                   scale=taps[:, b, 2 - b, bass.ds(ct, 1)]).then_inc(sem(f"{ph}_centre{half}"), 1)

            def nonlinear(i):
                act.wait_ge(sem(f"{ph}_conv0"), i * 8 + 8)
                act.activation(cvg[:, :, :], cvg[:, :, :], ACT.Silu if b else ACT.Gelu_apprx_tanh)\
                   .then_inc(sem(f"{ph}_nl"), 1)

            def body(i, first):
                for c in range(BODY):
                    s_hi(act, ph, i, BODY, c)
                    if c == 0 and not first:
                        nonlinear(i - 1)
                    if c == 3 and not first:
                        evacuate(i - 1, 1)
                    if c == 3 and first:
                        sumsq_act(act, ph, 2 * b + 1, x_sem, x_count)
                    if c == 5 and not first:
                        centre(i - 1, 1)
                    if c == CPG + 3:
                        if first:
                            act.wait_ge(sem(f"{ph}_rstd"), 1)
                        evacuate(i, 0)
                    if c == CPG + 5:
                        centre(i, 0)
            body(0, True)
            with act.Fori(1, FG) as i:
                body(i, False)
            nonlinear(FG - 1)
            evacuate(FG - 1, 1)
            centre(FG - 1, 1)

        def up_dve(dve, ph, b):
            cv = (cvg, cvu)

            def convolve(i, half):
                dve.wait_ge(sem(f"{ph}_centre{half}"), i * 4 + 4)
                for j, (tap, d) in enumerate((((1, 1), (0, 2)), ((0, 1), (2, -1)))[b]):
                    if j:
                        dve.wait_ge(sem(f"{ph}_conv{half}"), i * 8 + 4)
                    o = slice(d, S) if d > 0 else slice(0, S + d)
                    u = slice(0, S - d) if d > 0 else slice(-d, S)
                    for k in range(4):
                        ct = i * 4 + (half * FT + k)
                        dve.scalar_tensor_tensor(out=cv[half][:, k, o], in0=tp[half][:, k, u],
                                                 scalar=taps[:, b, tap, bass.ds(ct, 1)], in1=cv[half][:, k, o],
                                                 op0=ALU.mult, op1=ALU.add).then_inc(sem(f"{ph}_conv{half}"), 1)

            def body(i, first):
                for c in range(BODY):
                    s_lo(dve, ph, i, BODY, c)
                    if c == 3 and first:
                        sumsq_dve(dve, ph, 2 * b + 1)
                    if c == 6 and not first:
                        convolve(i - 1, 1)
                    if c == CPG + 6:
                        convolve(i, 0)
            body(0, True)
            with dve.Fori(1, FG) as i:
                body(i, False)
            convolve(FG - 1, 1)

        def up_pool(pool, ph):
            pool.memset(prime[:, :], 0.0).then_inc(sem(f"{ph}_hid"), 1)
            with pool.Fori(0, FG) as i:
                pool.wait_ge(sem(f"{ph}_nl"), i + 1)
                pool.wait_ge(sem(f"{ph}_conv1"), i * 8 + 8)
                pool.tensor_tensor(cvg[:, :, :], cvg[:, :, :], cvu[:, :, :], ALU.mult).then_inc(sem(f"{ph}_pr"), 1)
                pool.wait_ge(sem(f"{ph}_pr"), i + 1)
                pool.tensor_copy(hhi[:, bass.ds(i * 4, 4), :], cvg[:, :, :]).then_inc(sem(f"{ph}_hh"), 1)
                pool.wait_ge(sem(f"{ph}_hh"), i + 1)
                pool.tensor_tensor(hlo[:, bass.ds(i * 4, 4), :], cvg[:, :, :],
                                   hhi[:, bass.ds(i * 4, 4), :].bitcast(F32), ALU.subtract)\
                    .then_inc(sem(f"{ph}_hid"), 1)

        def bcast(ap, at, n):
            a = [list(d) for d in ap.ap]
            return bass.AP(tensor=ap.tensor, offset=ap.offset, ap=a[:at] + [[0, n]] + a[at:])

        def strided(ap, dims):
            return bass.AP(tensor=ap.tensor, offset=ap.offset, ap=[list(ap.ap[0])] + [list(d) for d in dims])

        par_in, mix_in = sem("par_in"), sem("mix_in")

        def setup_sp(sp):
            for q in range(4):
                c = slice(q * GC, (q + 1) * GC)
                sp.dma_start(x[:, :, c], T["x"][0][:, c].rearrange("(n p) c -> p n c", p=P)).then_inc(sem(f"x_in{q}"), 16)

        ROWS = [("pre_mix_norm", 0, 0), ("pre_ffn_norm", 0, KT), ("norm_pre_mix_2", 0, 2 * KT),
                ("norm_pre_ffn_2", 0, 3 * KT), ("cmp_pos_k", 0, 4 * KT), ("cmp_pos_v", 0, 4 * KT + CMP_L)]

        def setup_act(act):
            for name, j, r in ROWS:
                src = T[name].rearrange("a (r c) -> (a r) c", c=P) if "norm" in name else T[name][0]
                act.dma_start(pst[r:r + src.shape[0], j, :], src).then_inc(par_in, 16)
            for j in range(3):
                act.dma_start(pst[0:2 * FT, 1 + j, :], T["conv_w"][0, j].rearrange("(r c) -> r c", c=P)).then_inc(par_in, 16)
                act.dma_start(pst[0:2 * FT, 5 + j, :], T["ffn_w_conv_2"][0, j].rearrange("(r c) -> r c", c=P)).then_inc(par_in, 16)
            act.dma_start(pst[0:2 * FT, 4, :], T["conv_b"][0].rearrange("(r c) -> r c", c=P)).then_inc(par_in, 16)
            act.dma_start(tabaug[0:N_BUCKETS, :], T["rel_bias"]).then_inc(par_in, 16)
            act.dma_start(onehot[:, :], T["onehot"]).then_inc(par_in, 16)

        N_PAR = (len(ROWS) + 9) * 16

        def setup_pool(pool):
            pool.memset(ident[:, :], 0.0).then_inc(sem("ident"), 1)
            pool.wait_ge(sem("ident"), 1)
            pool.memset(tabaug[N_BUCKETS:N_BUCKETS + 1, :], NEG).then_inc(sem("ident"), 1)
            pool.wait_ge(sem("ident"), 2)
            pool.affine_select(out=ident[:, :], in_=ident[:, :], compare_op=ALU.not_equal, fill=1.0, base=0,
                               pattern=[[-1, P]], channel_multiplier=1).then_inc(sem("ident"), 1)
            pool.dma_start(wg[:, :, :], T["w_in"][0][:, G0:G0 + NGATE].rearrange("(k p) c -> p k c", p=P)).then_inc(mix_in, 16)
            for a, name in enumerate(("cmp_k_w2", "cmp_v_w2")):
                pool.dma_start(w2[:, a, :, :], T[name][0].rearrange("(k p) c -> p k c", p=P)).then_inc(mix_in, 16)
            pool.dma_start(cmask[:, :, :, :], T["cmask"]).then_inc(mix_in, 16)
            pool.dma_start(sub[:, :], bcast(T["diff_subln"][0], 0, P)).then_inc(mix_in, 16)
            for j, name in enumerate(("lambda_q1", "lambda_k1", "lambda_q2", "lambda_k2")):
                pool.dma_start(lam4[:, j, :], bcast(T[name][0], 0, P)).then_inc(mix_in, 16)
            pool.wait_ge(sem("toep"), 1)
            pool.dma_start(T["scratch"], bass.AP(tensor=toep, offset=0, ap=[[TOEP, 16], [0, P], [1, TOEP]]))\
                .then_inc(sem("skew_out"), 16)
            pool.wait_ge(sem("skew_out"), 16)
            t = T["scratch"]
            pool.dma_start(bias[:, :, :], bass.AP(tensor=t.tensor, offset=t.offset + P - 1,
                                                  ap=[[TOEP - 1, P], [P * TOEP, 16], [1, S]]))\
                .then_inc(sem("bias_in"), 16)

        N_MIX = 9 * 16

        def setup_pe(pe):
            pe.wait_ge(sem("ident"), 3)
            pe.wait_ge(par_in, N_PAR)
            for j in range(8):
                n = P if j == 0 else 2 * FT
                mm = pe.transpose(acc[0][:, j // 4, j % 4 * P:j % 4 * P + n], pst[0:n, j, :], ident[0:n, 0:n])
            mm.then_inc(sem("par_turned"), 1)
            pe.matmul(acc[1][0:16, 0, 0:TOEP], tabaug[:, :], onehot[:, :], start=True, stop=True)\
              .then_inc(sem("toep_sum"), 1)

        def setup_dve(dve):
            dve.memset(taps[:, 1, 3, :], 0.0)
            dve.wait_ge(sem("par_turned"), 1)
            a = acc[0]
            dve.tensor_copy(gains[:, :, :].rearrange("p a k -> p (a k)"), a[:, 0, 0:4 * KT]).then_inc(sem("par_ok"), 1)
            dve.tensor_copy(posT[:, :, :].rearrange("p a k -> p (a k)"), a[:, 0, 4 * KT:P]).then_inc(sem("par_ok"), 1)
            for j in range(1, 8):
                b, tap = (0, j - 1) if j < 5 else (1, j - 5)
                dve.tensor_copy(taps[:, b, tap, :], a[:, j // 4, j % 4 * P:j % 4 * P + 2 * FT]).then_inc(sem("par_ok"), 1)

        def in1_load(sp):
            w = T["w_in"][0]

            def body(i):
                for c in range(BODY):
                    s_load(sp, "in1", i, BODY, c, w_tile(w, CK * (c % CPG), i * (2 * GC) + c // CPG * GC))
            body(0)
            with sp.Fori(1, IN1 // 2) as i:
                body(i)
            for c in range(CPG):
                s_load(sp, "in1", IN1 // 2, BODY, c, w_tile(w, CK * c, (IN1 - 1) * GC))

        def in1_pe(pe):
            pe.wait_ge(sem("par_ok"), 9)
            pe.wait_ge(sem("toep"), 1)

            def half(i, h, ready=None):
                group(pe, h + i * 2)
                for c in range(CPG):
                    cc = h * CPG + c
                    products(pe, cb["in1"] + cc + i * BODY, cc % RING, acc[h], ahi, alo, CK * c, KT, ready)
            half(0, 0, "in1")
            half(0, 1)
            with pe.Fori(1, IN1 // 2) as i:
                half(i, 0)
                half(i, 1)
            half(IN1 // 2, 0)
            pe.wait_ge(sem("wg_lo"), 1)
            for t in range(NT):
                for kt in range(KT):
                    xh, xl = ahi[:, kt, t * P:(t + 1) * P], alo[:, kt, t * P:(t + 1) * P]
                    o = tp[0][:, 2 * t, 0:NGATE]
                    pe.matmul(o, xh, wghi[:, kt, :], start=(kt == 0), stop=False)
                    pe.matmul(o, xh, wglo[:, kt, :], start=False, stop=False)
                    mm = pe.matmul(o, xl, wghi[:, kt, :], start=False, stop=(kt == KT - 1))
            mm.then_inc(sem("gate_sum"), 1)

        def in1_act(act):
            act.wait_ge(sem("toep_sum"), 1)
            act.activation(toep[:, :], acc[1][0:16, 0, 0:TOEP], ACT.Copy).then_inc(sem("toep"), 1)
            act.wait_ge(sem("par_ok"), 1)
            pre_act(act, "in1", 0)

            def evacuate(i, h):
                act.wait_ge(chunk_used, cb["in1"] + CPG * (h + 1) + i * BODY)
                for t in range(NT):
                    m = act.activation(ptok[:, t, bass.ds(i * (2 * GC) + h * GC, GC)], acc[h][:, t, :], ACT.Copy,
                                       scale=rstd[:, 0, t:t + 1])
                m.then_inc(group_free, 1)

            def body(i, first):
                for c in range(BODY):
                    s_hi(act, "in1", i, BODY, c)
                    if first and c == 3:
                        sumsq_act(act, "in1", 0, sem("x_in3"), 16)
                        act.wait_ge(mix_in, N_MIX)
                        act.activation(wghi[:, :, :], wg[:, :, :], ACT.Copy).then_inc(sem("wg_hi"), 1)
                        act.wait_ge(sem("in1_rstd"), 1)
                    if not first and c == 3:
                        evacuate(i - 1, 1)
                    if c == CPG + 3:
                        evacuate(i, 0)
            body(0, True)
            with act.Fori(1, IN1 // 2) as i:
                body(i, False)
            for c in range(CPG):
                s_hi(act, "in1", IN1 // 2, BODY, c)
                if c == 3:
                    evacuate(IN1 // 2 - 1, 1)
            evacuate(IN1 // 2, 0)
            act.wait_ge(sem("gate_sum"), 1)
            for t in range(NT):
                act.activation(gate[:, t, :], tp[0][:, 2 * t, 0:NGATE], ACT.Sigmoid, scale=rstd[:, 0, t:t + 1])\
                   .then_inc(sem("gate"), 1)
            act.wait_ge(sem("lam_sum"), 2)
            act.activation(lamv[:, 2:4], lamv[:, 0:2], ACT.Exp).then_inc(sem("lam_exp"), 1)

        def in1_dve(dve):
            pre_dve(dve, "in1", 0)

            def body(i, first):
                for c in range(BODY):
                    s_lo(dve, "in1", i, BODY, c)
                    if first and c == 3:
                        sumsq_dve(dve, "in1", 0)
                        dve.wait_ge(sem("wg_hi"), 1)
                        dve.tensor_tensor(wglo[:, :, :], wg[:, :, :], wghi[:, :, :].bitcast(F32), ALU.subtract)\
                           .then_inc(sem("wg_lo"), 1)
                        dve.wait_ge(mix_in, N_MIX)
                        dve.tensor_tensor(lam4[:, 0:3:2, :], lam4[:, 0:3:2, :], lam4[:, 1:4:2, :], ALU.mult)\
                           .then_inc(sem("lam_sum"), 1)
                        dve.wait_ge(sem("lam_sum"), 1)
                        dve.tensor_reduce(lamv[:, 0:2], lam4[:, 0:3:2, :], AX.X, ALU.add).then_inc(sem("lam_sum"), 1)
                        dve.tensor_scalar(sub[:, :], sub[:, :], 1.0 - LAM_INIT, None, ALU.mult).then_inc(sem("sub"), 1)
            body(0, True)
            with dve.Fori(1, IN1 // 2) as i:
                body(i, False)
            for c in range(CPG):
                s_lo(dve, "in1", IN1 // 2, BODY, c)
            dve.wait_ge(sem("lam_exp"), 1)
            dve.scalar_tensor_tensor(out=lamv[:, 4:5], in0=lamv[:, 3:4], scalar=-LAM_INIT, in1=lamv[:, 2:3],
                                     op0=ALU.add, op1=ALU.subtract).then_inc(sem("nlam"), 1)

        UNITS = 2 * (DIFF_H + NSA_H)

        def unit(u):
            return (u % 16) // 2, u % 2, P * (u % 2 + 1)

        CA = "cmp"

        def m1_load(sp):
            for a, name in enumerate(("cmp_k_w1", "cmp_v_w1")):
                for c in range(CMP_CH):
                    src = T[name][0][c * CMP_LPC * P:(c + 1) * CMP_LPC * P, :].rearrange("(k p) c -> p k c", p=P)
                    s_load(sp, CA, 0, 0, a * CMP_CH + c, src, CMP_LPC)

        def m1_pe(pe):
            pe.wait_ge(group_free, IN1)
            for b in range(8):
                if b == 1:
                    pe.wait_ge(sem("gate"), NT)
                if b >= 2:
                    pe.wait_ge(sem(f"m1_turn_read{b % 2}"), b // 2)
                for k in range(4):
                    for t in range(NT):
                        c = TURN[4 * b + k]
                        mm = pe.transpose(tp[(b + 1) % 2][:, k, t * P:(t + 1) * P], ptok[:, t, c:c + P], ident[:, :])
                mm.then_inc(sem("m1_turned"), 1)
            for a in range(2):
                pe.wait_ge(sem("blk_lo"), a + 1)
                for c in range(CMP_CH):
                    n = cb[CA] + a * CMP_CH + c
                    pe.wait_ge(lo_done, n + 1)
                    for k in range(CMP_LPC):
                        l = c * CMP_LPC + k
                        for ht in range(2):
                            o = acc[a][:, ht, 0:NCG]
                            cc = slice(k * HID + ht * P, k * HID + (ht + 1) * P)
                            pe.matmul(o, whi[:, n % RING, cc], blkhi[:, a, l, :], start=(l == 0), stop=False)
                            pe.matmul(o, whi[:, n % RING, cc], blklo[:, a, l, :], start=False, stop=False)
                            mm = pe.matmul(o, wlo[:, n % RING, cc], blkhi[:, a, l, :], start=False,
                                           stop=(l == CMP_L - 1))
                    mm.then_inc(chunk_used, 1)
            pe.wait_ge(sem("cmp_hid"), 4)
            for ht in range(2):
                pe.matmul(acc[0][:, 0, 0:NCG], w2[:, 0, ht, :], hidT[:, 0, ht, :], start=(ht == 0), stop=(ht == 1))
            for g in range(NSA_KV):
                for ht in range(2):
                    mm = pe.matmul(acc[0][0:NC_, 1, g * P:(g + 1) * P], hidT[:, 1, ht, g * NC_:(g + 1) * NC_],
                                   w2[:, 1, ht, :], start=(ht == 0), stop=(ht == 1))
            mm.then_inc(sem("cmp_kv"), 1)
            pe.wait_ge(sem("cmp_kv_ok"), 2)
            for qt in range(NT):
                for h in range(NSA_H):
                    g, c = h // NSA_GROUP, (qt * NSA_H + h) * NC_
                    mm = pe.matmul(acc[1][:, 0, c:c + NC_], qkT[:, T_NQ + h, qt * P:(qt + 1) * P],
                                   kcmpT[:, g * NC_:(g + 1) * NC_], start=True, stop=True)
            mm.then_inc(sem("cmp_sc"), 1)

            def scores(u):
                h, qt, nk = unit(u)
                if u < 2:
                    pe.wait_ge(sem("pc_sc"), 2)
                else:
                    pe.wait_ge(sem("m1_sb"), u - 1)
                for m in range(2):
                    if u < 16:
                        r = slice(64 * m, 64 * m + 64)
                        q, k = qkT[r, T_DQ + h, qt * P:(qt + 1) * P], qkT[r, T_DK + h, 0:nk]
                    else:
                        q = qkT[:, T_NQ + h, qt * P:(qt + 1) * P]
                        k = qkT[:, (T_KS, T_KW)[m] + h // NSA_GROUP, 0:nk]
                    mm = pe.matmul(acc[u % 2][:, m, 0:nk], q, k, start=True, stop=True)
                mm.then_inc(sem("m1_sc"), 1)

            def flat(u):
                return tp[u % 2][:, :, :].rearrange("p k t -> p (k t)")

            def turn(u):
                h, qt, nk = unit(u)
                if u >= 2:
                    pe.wait_ge(sem("m1_o"), u - 1)
                else:
                    pe.wait_ge(sem(f"m1_turn_read{1 - u}"), 4)
                pe.wait_ge(sem("m1_p"), u + 1)
                if u >= 16:
                    pe.wait_ge(sem("pc"), 1)
                for m in range(1 if u < 16 else 2):
                    for kt in range(nk // P):
                        c = m * nk + kt * P
                        mm = pe.transpose(flat(u)[:, c:c + P], prb[u % 2][:, m, kt * P:(kt + 1) * P], ident[:, :])
                if u >= 16:
                    mm = pe.transpose(flat(u)[0:NC_, 2 * nk:2 * nk + P], pc[:, qt, h, :], ident[:, :])
                mm.then_inc(sem("m1_turned"), 1)

            def weighted(u):
                h, qt, nk = unit(u)
                o = flat(u)[:, 7 * P:8 * P]
                pe.wait_ge(sem("m1_pt"), u + 1)
                t = pts[u % 2]
                if u < 16:
                    for kt in range(nk // P):
                        mm = pe.matmul(o, t[:, kt * P:(kt + 1) * P], ptok[:, kt, DV + h * P:DV + (h + 1) * P],
                                       start=(kt == 0), stop=(kt == nk // P - 1))
                else:
                    g = h // NSA_GROUP
                    for m, v in enumerate((VS, VW)):
                        for kt in range(nk // P):
                            c = m * nk + kt * P
                            pe.matmul(o, t[:, c:c + P], ptok[:, kt, v + g * P:v + (g + 1) * P],
                                      start=(m == 0 and kt == 0), stop=False)
                    mm = pe.matmul(o, t[0:NC_, 2 * nk:2 * nk + P], vcmp[:, g, :], start=False, stop=True)
                mm.then_inc(sem("m1_pv"), 1)

            scores(0)
            scores(1)
            for u in range(UNITS):
                if u + 2 < UNITS:
                    scores(u + 2)
                turn(u)
                if u >= 1:
                    weighted(u - 1)
            weighted(UNITS - 1)

        def m1_act(act):
            act.wait_ge(sem("skew_out"), 16)
            for b in range(0, 8, 2):
                act.wait_ge(sem("m1_turned"), b + 1)
                act.activation(qkT[:, 4 * b:4 * b + 4, :], tp[1][:, :, :], ACT.Copy).then_inc(sem("m1_turn_read0"), 1)
                if b == 0:
                    for a in range(2):
                        act.wait_ge(sem("blk"), 4 * a + 4)
                        act.activation(blkhi[:, a, :, :], blk[:, a, :, :], ACT.Copy).then_inc(sem("blk_hi"), 1)
            for c in range(2 * CMP_CH):
                s_hi(act, CA, 0, 0, c)
            for a in range(2):
                act.wait_ge(chunk_used, cb[CA] + (a + 1) * CMP_CH)
                for ht in range(2):
                    act.activation(hidT[:, a, ht, :], acc[a][:, ht, 0:NCG], ACT.Gelu_apprx_tanh)\
                       .then_inc(sem("cmp_hid"), 1)
            act.wait_ge(sem("cmp_kv"), 1)
            act.activation(kcmpT[:, :], acc[0][:, 0, 0:NCG], ACT.Copy).then_inc(sem("cmp_kv_ok"), 1)
            act.activation(vcmp[:, :, :].rearrange("p g c -> p (g c)"), acc[0][0:NC_, 1, 0:2 * P], ACT.Copy)\
               .then_inc(sem("cmp_kv_ok"), 1)
            act.wait_ge(sem("pc_sub"), 1)
            act.activation(pc[:, :, :, :], pc[:, :, :, :], ACT.Exp).then_inc(sem("pc_exp"), 1)

            def flat(u):
                return tp[u % 2][:, :, :].rearrange("p k t -> p (k t)")

            def exps(u):
                h, qt, nk = unit(u)
                act.wait_ge(sem("m1_max"), u + 1)
                if u >= 2:
                    act.wait_ge(sem("m1_turned"), 8 + u - 1)
                for m in range(2):
                    act.activation(prb[u % 2][:, m, 0:nk], scb[u % 2][:, m, 0:nk], ACT.Exp,
                                   bias=nmx[:, u, m:m + 1], accum_out=psm[:, u, m:m + 1]).then_inc(sem("m1_e"), 1)

            def turned(u):
                h, qt, nk = unit(u)
                act.wait_ge(sem("m1_turned"), 8 + u + 1)
                if u >= 2:
                    act.wait_ge(sem("m1_pv"), u - 1)
                if u < 16:
                    m = act.activation(pts[u % 2][:, 0:nk], flat(u)[:, 0:nk], ACT.Copy)
                else:
                    act.activation(pts[u % 2][0:NC_, 2 * nk:2 * nk + P], flat(u)[0:NC_, 2 * nk:2 * nk + P], ACT.Copy)
                    m = act.activation(pts[u % 2][:, 0:2 * nk], flat(u)[:, 0:2 * nk], ACT.Copy)
                m.then_inc(sem("m1_pt"), 1)

            def outs(u):
                h, qt, nk = unit(u)
                o = flat(u)[:, 7 * P:8 * P]
                act.wait_ge(sem("m1_pv"), u + 1)
                c = (0 if u < 16 else DIFF_H * P) + h * P
                m = act.activation(mix1[:, qt, c:c + P], o, ACT.Copy)
                if u < 16:
                    m = act.activation(o, o, ACT.Square, accum_out=dsq[:, qt, h:h + 1])
                m.then_inc(sem("m1_o"), 1)

            exps(0)
            for u in range(UNITS):
                if u + 1 < UNITS:
                    exps(u + 1)
                turned(u)
                if u >= 1:
                    outs(u - 1)
                if u == 18:
                    act.wait_ge(sem("d_ms"), 1)
                    act.activation(drs[:, :, :], dsq[:, :, :], ACT.Sqrt).then_inc(sem("d_root"), 1)
            outs(UNITS - 1)

        def m1_dve(dve):
            dve.wait_ge(sem("skew_out"), 16)
            for b in range(8):
                if b % 2:
                    dve.wait_ge(sem("m1_turned"), b + 1)
                    dve.tensor_copy(qkT[:, 4 * b:4 * b + 4, :], tp[0][:, :, :]).then_inc(sem("m1_turn_read1"), 1)
                if b == 1:
                    dve.wait_ge(sem("m1_turn_read0"), 1)
                    for a in range(2):
                        for g in range(NSA_KV):
                            for lh in range(2):
                                l0 = lh * CMP_STRIDE
                                t = qkT[:, (T_KC, T_VC)[a] + g, l0:l0 + 1]
                                dve.tensor_tensor(
                                    blk[:, a, l0:l0 + CMP_STRIDE, g * NC_:(g + 1) * NC_],
                                    strided(t, [[1, CMP_STRIDE], [CMP_STRIDE, NC_]]),
                                    strided(posT[:, a, l0:l0 + 1], [[1, CMP_STRIDE], [0, NC_]]), ALU.add)\
                                   .then_inc(sem("blk"), 1)
                    for a in range(2):
                        dve.wait_ge(sem("blk_hi"), a + 1)
                        dve.wait_ge(sem("blk"), 4 * a + 4)
                        dve.tensor_tensor(blklo[:, a, :, :], blk[:, a, :, :], blkhi[:, a, :, :].bitcast(F32),
                                          ALU.subtract).then_inc(sem("blk_lo"), 1)
            for c in range(2 * CMP_CH):
                s_lo(dve, CA, 0, 0, c)
            dve.wait_ge(sem("cmp_sc"), 1)
            for qt in range(NT):
                s_ = acc[1][:, 0, qt * NSA_H * NC_:(qt + 1) * NSA_H * NC_].rearrange("p (h c) -> p h c", h=NSA_H)
                dve.scalar_tensor_tensor(out=pc[:, qt, :, :], in0=s_, scalar=P ** -0.5,
                                         in1=bcast(cmask[:, 1, qt, :], 1, NSA_H), op0=ALU.mult, op1=ALU.add)\
                   .then_inc(sem("pc_sc"), 1)
            w_ = pc[:, :, :, :].rearrange("p n h c -> p (n h) c")
            st = [pcs[:, j, :, :].rearrange("p n h -> p (n h)") for j in range(4)]

            def wide(a):
                return bcast(a, 2, NC_)
            dve.wait_ge(sem("pc_sc"), 2)
            dve.tensor_reduce(st[0], w_, AX.X, ALU.max).then_inc(sem("pc_max"), 1)
            dve.wait_ge(sem("pc_max"), 1)
            dve.tensor_tensor(w_, w_, wide(st[0]), ALU.subtract).then_inc(sem("pc_sub"), 1)
            dve.wait_ge(sem("pc_exp"), 1)
            for qt in range(NT):
                dve.tensor_tensor(pc[:, qt, :, :], pc[:, qt, :, :], bcast(cmask[:, 0, qt, :], 1, NSA_H), ALU.mult)\
                   .then_inc(sem("pc_mask"), 1)
            dve.wait_ge(sem("pc_mask"), 2)
            dve.tensor_reduce(st[1], w_, AX.X, ALU.add).then_inc(sem("pc_st"), 1)
            dve.wait_ge(sem("pc_st"), 1)
            dve.tensor_scalar(st[1], st[1], TINY, None, ALU.max).then_inc(sem("pc_st"), 1)
            dve.wait_ge(sem("pc_st"), 2)
            dve.reciprocal(st[2], st[1]).then_inc(sem("pc_st"), 1)
            dve.wait_ge(sem("pc_st"), 3)
            dve.wait_ge(sem("gate"), NT)
            dve.tensor_tensor(pcs[:, 3, :, :], pcs[:, 2, :, :], gate[:, :, 0:NGATE:3], ALU.mult).then_inc(sem("pc_st"), 1)
            dve.wait_ge(sem("pc_st"), 4)
            dve.tensor_tensor(w_, w_, wide(st[3]), ALU.mult).then_inc(sem("pc"), 1)
            dve.wait_ge(sem("bias_in"), 16)
            dve.wait_ge(sem("nlam"), 1)

            def soft(u):
                h, qt, nk = unit(u)
                dve.wait_ge(sem("m1_sc"), u + 1)
                if u >= 2:
                    dve.wait_ge(sem("m1_e"), 2 * u - 2)
                b = bias[:, h + (0 if u < 16 else DIFF_H), S - nk:S]
                dve.scalar_tensor_tensor(out=scb[u % 2][:, :, 0:nk], in0=acc[u % 2][:, :, 0:nk],
                                         scalar=(64 if u < 16 else P) ** -0.5, in1=bcast(b, 1, 2),
                                         op0=ALU.mult, op1=ALU.add).then_inc(sem("m1_sb"), 1)
                dve.wait_ge(sem("m1_sb"), u + 1)
                dve.tensor_reduce(nmx[:, u, :], scb[u % 2][:, :, 0:nk], AX.X, ALU.max, negate=True)\
                   .then_inc(sem("m1_max"), 1)

            def weights(u):
                h, qt, nk = unit(u)
                p = prb[u % 2]
                dve.wait_ge(sem("m1_e"), 2 * u + 2)
                dve.reciprocal(cof[:, u, :], psm[:, u, :]).then_inc(sem("m1_rc"), 1)
                dve.wait_ge(sem("m1_rc"), u + 1)
                if u < 16:
                    dve.tensor_tensor(cof[:, u, 1:2], cof[:, u, 1:2], lamv[:, 4:5], ALU.mult).then_inc(sem("m1_cf"), 1)
                    dve.tensor_scalar(p[:, 0, 0:nk], p[:, 0, 0:nk], cof[:, u, 0:1], None, ALU.mult)\
                       .then_inc(sem("m1_cf"), 1)
                    dve.wait_ge(sem("m1_cf"), 2 * u + 2)
                    dve.scalar_tensor_tensor(out=p[:, 0, 0:nk], in0=p[:, 1, 0:nk], scalar=cof[:, u, 1:2],
                                             in1=p[:, 0, 0:nk], op0=ALU.mult, op1=ALU.add).then_inc(sem("m1_p"), 1)
                else:
                    dve.tensor_tensor(cof[:, u, :], cof[:, u, :], gate[:, qt, 3 * h + 1:3 * h + 3], ALU.mult)\
                       .then_inc(sem("m1_cg"), 1)
                    dve.wait_ge(sem("m1_cg"), u - 15)
                    dve.tensor_scalar(p[:, 0, 0:nk], p[:, 0, 0:nk], cof[:, u, 0:1], None, ALU.mult)
                    dve.tensor_scalar(p[:, 1, 0:nk], p[:, 1, 0:nk], cof[:, u, 1:2], None, ALU.mult)\
                       .then_inc(sem("m1_p"), 1)

            soft(0)
            for u in range(UNITS):
                if u + 1 < UNITS:
                    soft(u + 1)
                weights(u)
                if u == 17:
                    dve.wait_ge(sem("m1_o"), 16)
                    dve.tensor_scalar(dsq[:, :, :], dsq[:, :, :], 1.0 / P, EPS, ALU.mult, ALU.add)\
                       .then_inc(sem("d_ms"), 1)
                if u == 20:
                    dve.wait_ge(sem("d_root"), 1)
                    dve.reciprocal(drs[:, :, :], drs[:, :, :]).then_inc(sem("d_rs"), 1)
                    dve.wait_ge(sem("d_rs"), 1)
                    for t in range(NT):
                        o = mix1[:, t, 0:DIFF_H * P].rearrange("p (h c) -> p h c", h=DIFF_H)
                        dve.tensor_tensor(o, o, bcast(drs[:, t, :], 2, P), ALU.mult).then_inc(sem("d_n"), 1)
                if u in (22, 24):
                    t = (u - 22) // 2
                    o = mix1[:, t, 0:DIFF_H * P].rearrange("p (h c) -> p h c", h=DIFF_H)
                    dve.wait_ge(sem("d_n"), 2)
                    dve.tensor_tensor(o, o, bcast(sub[:, :], 1, DIFF_H), ALU.mult).then_inc(sem("m1_diff"), 1)

        def mix1_ready(pe, q):
            if q == 0:
                pe.wait_ge(sem("m1_diff"), 2)
                pe.wait_ge(sem("m1_o"), UNITS)

        H2 = "in2"

        def m2_load(sp):
            w = T["hgrn_w_in_2"][0]
            with sp.Fori(0, HJ) as i:
                for c in range(HCH):
                    s_load(sp, H2, i, HCH, c, w_tile(w, CK * (c % CPG), i * GC + c // CPG * D))

        def small(level):
            b = tp[1][:, :, :].rearrange("p k t -> p (k t)")
            return b[:, level % 2 * GC:(level % 2 + 1) * GC] if level < N_STEP - 1 else b

        UPS = 6 + 4 * (N_LEV - 2)

        def m2_pe(pe):
            def turn(i, j):
                pe.wait_ge(group_free, gb[H2] + j + 1 + i * HGRP)
                if j:
                    pe.wait_ge(sem("m2_t_read"), i * 3 + j)
                for k in range(HPG):
                    for t in range(NT):
                        mm = pe.transpose(tp[0][:, k, t * P:(t + 1) * P], stg[:, j, t, k * P:(k + 1) * P], ident[:, :])
                mm.then_inc(sem("m2_turned"), 1)

            def step(i, s):
                pe.wait_ge(sem("m2_dec"), i * N_STEP + s + 1)
                if s == N_STEP - 1:
                    pe.wait_ge(sem("m2_lev0"), i * 4 + 4)
                    pe.wait_ge(sem("m2_lev1"), i * 4 + 4)
                elif s >= 2:
                    pe.wait_ge(sem(f"m2_lev{s % 2}"), i * 4 + s // 2)
                q, k = (qT if s == 0 else qd[s % 2]), kd[s % 2]
                if s < 7:
                    for hd in range(HPG):
                        for t in range(NT):
                            for j in range(4):
                                jt = j ^ 1 if s == 6 else j
                                c = (hd * NT + t) * 32
                                mm = pe.matmul(small(s)[32 * j:32 * j + 32, c:c + 32],
                                               k[:, hd, t * P + 32 * j:t * P + 32 * j + 32],
                                               q[:, hd, t * P + 32 * jt:t * P + 32 * jt + 32], start=True, stop=True)
                elif s == 7:
                    for hd in range(HPG):
                        for t in range(NT):
                            for a in range(2):
                                c = (hd * NT + t) * 64
                                mm = pe.matmul(small(s)[64 * a:64 * a + 64, c:c + 64],
                                               k[:, hd, t * P + 64 * a:t * P + 64 * a + 64],
                                               q[:, hd, t * P + 64 * (1 - a):t * P + 64 * (2 - a)],
                                               start=True, stop=True)
                else:
                    for hd in range(HPG):
                        for t in range(NT):
                            c = (hd * NT + t) * P
                            mm = pe.matmul(small(s)[:, c:c + P], k[:, hd, t * P:(t + 1) * P],
                                           q[:, hd, (1 - t) * P:(2 - t) * P], start=True, stop=True)
                mm.then_inc(sem("m2_step"), 1)

            def outs(i):
                pe.wait_ge(sem("m2_at"), i + 1)
                o = small(N_STEP - 1)
                for t in range(NT):
                    for hd in range(HPG):
                        c = (t * HPG + hd) * P
                        for s in range(NT):
                            mm = pe.matmul(o[:, c:c + P], at[:, hd, s, t * P:(t + 1) * P],
                                           vt[:, s, hd * P:(hd + 1) * P], start=(s == 0), stop=(s == NT - 1))
                mm.then_inc(sem("m2_pv"), 1)

            def body(i, first):
                for c in range(HCH):
                    if c == 0:
                        pe.wait_ge(group_free, gb[H2] + i * HGRP)
                    elif c % CPG == 0:
                        group(pe, gb[H2] + c // CPG + i * HGRP)
                    products(pe, cb[H2] + c + i * HCH, c % RING, acc[c // CPG % 2], ahi, alo, CK * (c % CPG), KT,
                             "in2" if first and c < CPG else None)
                    if c in (10, 18, 26):
                        turn(i, c // CPG - 1)
                    if c == 31:
                        step(i, 0)
                    if c in (31, 34, 37):
                        step(i, 1 + (c - 31) // 3)
                    if not first and c in (0, 3, 6, 9, 12):
                        step(i - 1, 4 + c // 3)
                    if not first and c == 15:
                        outs(i - 1)
            body(0, True)
            with pe.Fori(1, HJ) as i:
                body(i, False)
            for s in range(4, N_STEP):
                step(HJ - 1, s)
            outs(HJ - 1)

        def m2_act(act):
            def full(i, g):
                act.wait_ge(chunk_used, cb[H2] + CPG * (g + 1) + i * HCH)

            def evacuate(i, g):
                full(i, g)
                for t in range(NT):
                    dst = sgm[:, t, :] if g in (0, 4) else vt[:, t, :] if g == 3 else stg[:, g, t, :]
                    m = act.activation(dst, acc[g % 2][:, t, :], ACT.Copy if g == 3 else ACT.Sigmoid,
                                       scale=rstd[:, 2, t:t + 1])
                m.then_inc(sem("m2_sig") if g in (0, 4) else group_free, 1)

            def turned(i, j, first):
                act.wait_ge(sem("m2_turned"), i * 3 + (j + 1))
                if j == 0 and not first:
                    act.wait_ge(sem("m2_dec"), i * N_STEP)
                act.activation((qT, pf, ib)[j][:, :, :], tp[0][:, :, :], ACT.Copy)\
                   .then_inc(sem("m2_cp") if j else sem("m2_t_read"), 1)

            def level(i, s):
                act.wait_ge(sem("m2_step"), i * N_STEP + s + 1)
                if s == 6:
                    for j in range(4):
                        r = slice(32 * j, 32 * j + 32)
                        m = act.activation(strided(at[r, 0, 0, 32 * (j ^ 1):32 * (j ^ 1) + 1], [[NT * S, HPG], [S + P, NT], [1, 32]]),
                                           small(6)[r, 0:HPG * NT * 32].rearrange("p (a b c) -> p a b c", a=HPG, b=NT),
                                           ACT.Copy)
                    m.then_inc(sem("m2_lev0"), 1)
                elif s == 7:
                    for a in range(2):
                        r = slice(64 * a, 64 * a + 64)
                        m = act.activation(strided(at[r, 0, 0, 64 * (1 - a):64 * (1 - a) + 1], [[NT * S, HPG], [S + P, NT], [1, 64]]),
                                           small(7)[r, 0:HPG * NT * 64].rearrange("p (a b c) -> p a b c", a=HPG, b=NT),
                                           ACT.Copy)
                    m.then_inc(sem("m2_lev1"), 1)
                else:
                    act.activation(strided(at[:, 0, 0, P:P + 1], [[NT * S, HPG], [P, NT], [1, P]]),
                                   small(8).rearrange("p (a b c) -> p a b c", a=HPG, b=NT), ACT.Copy)\
                       .then_inc(sem("m2_at"), 1)

            def diagonal(i):
                act.wait_ge(sem("m2_lev1"), i * 4 + 3)
                for j in range(4):
                    r = slice(32 * j, 32 * j + 32)
                    act.activation(strided(at[r, 0, 0, 32 * j:32 * j + 1], [[NT * S, HPG], [S + P, NT], [1, 32]]),
                                   ad[r, :, :, :], ACT.Copy)

            def squares(i):
                act.wait_ge(sem("m2_pv"), i + 1)
                act.activation(sgm[:, :, :].rearrange("p n c -> p (n c)"), small(N_STEP - 1), ACT.Square)\
                   .then_inc(sem("m2_sq"), 1)

            def tail(i, c):
                if c == 3:
                    evacuate(i, 4)
                if c == 7:
                    diagonal(i)
                if c in (8, 11, 14):
                    level(i, 6 + (c - 8) // 3)
                if c == 17:
                    squares(i)

            def body(i, first):
                for c in range(HCH):
                    s_hi(act, H2, i, HCH, c)
                    if c == 3 and first:
                        sumsq_act(act, "in2", 2, sem("down1_x"), 8)
                        act.wait_ge(sem("in2_rstd"), 1)
                    if not first:
                        tail(i - 1, c)
                    if c in (11, 19, 27, 35):
                        evacuate(i, (c - 11) // 8)
                    if c in (12, 20, 28):
                        turned(i, (c - 12) // 8, first)
            body(0, True)
            with act.Fori(1, HJ) as i:
                body(i, False)
            for c in range(18):
                tail(HJ - 1, c)
            act.wait_ge(sem("h_ms"), 1)
            act.activation(hrs[:, :, :], hsq[:, :, :], ACT.Sqrt).then_inc(sem("h_root"), 1)

        def m2_dve(dve):
            def halves(a, h):
                v = a[:, :, :].rearrange("p q (n two h) -> p (q n) two h", two=2, h=h)
                return v[:, :, 0, :], v[:, :, 1, :]

            def silu(i, g, dst):
                dve.wait_ge(sem("m2_sig"), i * 2 + (1 if g == 0 else 2))
                for t in range(NT):
                    m = dve.scalar_tensor_tensor(out=dst[:, t, :], in0=acc[0][:, t, :], scalar=rstd[:, 2, t:t + 1],
                                                 in1=sgm[:, t, :], op0=ALU.mult, op1=ALU.mult)
                m.then_inc(group_free, 1)

            def keys(i, j):
                dve.wait_ge(sem("m2_cp"), i * 2 + j)
                dve.tensor_scalar((kf, kb)[j - 1][:, :, :], tp[0][:, :, :], -1.0, 1.0, ALU.mult, ALU.add)\
                   .then_inc(sem("m2_t_read"), 1)

            def decay(i, s):
                if s >= 2:
                    dve.wait_ge(sem("m2_step"), i * N_STEP + s - 1)
                if s == 0:
                    dve.wait_ge(sem("m2_t_read"), i * 3 + 3)
                    dve.tensor_tensor(kd[0][:, :, :], kf[:, :, :], kb[:, :, :], ALU.add).then_inc(sem("m2_dec"), 1)
                    return
                h = 2 ** (s - 1)
                up = sem("m2_up")
                (q1, q2), (kf1, _), (_, kb2) = halves(qT, h), halves(kf, h), halves(kb, h)
                (pf1, pf2), (sf1, sf2) = halves(pf, h), halves(sf, h)
                (ib1, ib2), (eb1, eb2) = halves(ib, h), halves(eb, h)
                (qd1, qd2), (kd1, kd2) = halves(qd[s % 2], h), halves(kd[s % 2], h)
                if h == 1:
                    dve.tensor_copy(kd1, kf1)
                    dve.tensor_copy(kd2, kb2)
                else:
                    dve.wait_ge(up, i * UPS + 6 + 4 * (s - 2))
                    dve.tensor_tensor(kd1, kf1, sf1, ALU.mult)
                    dve.tensor_tensor(kd2, kb2, eb2, ALU.mult)
                dve.tensor_tensor(qd2, q2, pf2, ALU.mult)
                dve.tensor_tensor(qd1, q1, ib1, ALU.mult).then_inc(sem("m2_dec"), 1)
                if h == S // 2:
                    return
                pl1, pl2 = pf1[:, :, h - 1:h], pf2[:, :, h - 1:h]
                il1, il2 = ib1[:, :, 0:1], ib2[:, :, 0:1]

                def over(a):
                    b = [list(d) for d in a.ap]
                    return bass.AP(tensor=a.tensor, offset=a.offset, ap=b[:-1] + [[0, h]])
                if h == 1:
                    dve.memset(sf2, 1.0).then_inc(up, 1)
                    dve.memset(eb1, 1.0).then_inc(up, 1)
                    dve.tensor_copy(sf1, pf2).then_inc(up, 1)
                    dve.tensor_copy(eb2, ib1).then_inc(up, 1)
                else:
                    dve.tensor_tensor(sf1, sf1, over(pl2), ALU.mult).then_inc(up, 1)
                    dve.tensor_tensor(eb2, eb2, over(il1), ALU.mult).then_inc(up, 1)
                dve.wait_ge(up, i * UPS + (4 if h == 1 else 4 * s))
                dve.tensor_tensor(pf2, pf2, over(pl1), ALU.mult).then_inc(up, 1)
                dve.tensor_tensor(ib1, ib1, over(il2), ALU.mult).then_inc(up, 1)

            def level(i, s):
                dve.wait_ge(sem("m2_step"), i * N_STEP + s + 1)
                if s == 0:
                    dve.tensor_tensor(ad[:, :, :, :].rearrange("p a b c -> p (a b) c"),
                                      small(0)[:, 0:HPG * NT * 32].rearrange("p (a c) -> p a c", c=32),
                                      bcast(lmask[:, 5, :], 1, HPG * NT), ALU.mult).then_inc(sem("m2_lev0"), 1)
                    return
                else:
                    dve.wait_ge(sem(f"m2_lev{(s - 1) % 2}"), i * 4 + (s - 1) // 2 + 1)
                dve.tensor_tensor(lpick[:, :, :], small(s)[:, 0:HPG * NT * 32].rearrange("p (a c) -> p a c", c=32),
                                  bcast(lmask[:, s - 1, :], 1, HPG * NT), ALU.mult).then_inc(sem("m2_pick"), 1)
                dve.wait_ge(sem("m2_pick"), i * 5 + s)
                a = ad[:, :, :, :].rearrange("p a b c -> p (a b) c")
                dve.tensor_tensor(a, a, lpick[:, :, :], ALU.add).then_inc(sem(f"m2_lev{s % 2}"), 1)

            def outputs(i):
                dve.wait_ge(sem("m2_pv"), i + 1)
                o = small(N_STEP - 1).rearrange("p (n c) -> p n c", n=NT)
                dve.wait_ge(sem("m2_sq"), i + 1)
                dve.tensor_tensor(mix2[:, :, bass.ds(i * GC, GC)], o, gs[:, :, :], ALU.mult)
                dve.tensor_reduce(hsq[:, :, bass.ds(i * HPG, HPG)],
                                  sgm[:, :, :].rearrange("p n (h c) -> p n h c", c=P), AX.X, ALU.add)\
                   .then_inc(sem("m2_o"), 1)

            def tail(i, c):
                if c == 1:
                    silu(i, 4, gs)
                if c == 5:
                    dve.wait_ge(group_free, gb[H2] + HGRP + i * HGRP)
                    g4 = gs[:, :, :].rearrange("p n (h c) -> p (n h) c", c=P)
                    dve.tensor_tensor(g4, g4, bcast(gnb[:, :], 1, NT * HPG), ALU.mult).then_inc(sem("m2_gs"), 1)
                if c in (1, 4, 7, 10):
                    decay(i, 5 + c // 3)
                if c in (2, 5):
                    level(i, 4 + c // 3)
                if c == 17:
                    dve.wait_ge(sem("m2_gs"), i + 1)
                    outputs(i)

            def body(i, first):
                for c in range(HCH):
                    s_lo(dve, H2, i, HCH, c)
                    if c == 3 and first:
                        sumsq_dve(dve, "in2", 2)
                        dve.wait_ge(sem("in2_rstd"), 1)
                        dve.wait_ge(sem("m2_gn"), 32)
                    if not first:
                        tail(i - 1, c)
                    if c == 11:
                        silu(i, 0, stg[:, 0, :, :])
                    if c in (20, 28):
                        keys(i, 1 + (c - 20) // 8)
                    if c == 29:
                        decay(i, 0)
                    if c in (29, 32, 35, 38):
                        decay(i, 1 + (c - 29) // 3)
                    if c == 33:
                        level(i, 0)
                    if c in (34, 37):
                        level(i, 1 + (c - 34) // 3)
                    if c == 39:
                        level(i, 3)
            body(0, True)
            with dve.Fori(1, HJ) as i:
                body(i, False)
            for c in range(18):
                tail(HJ - 1, c)
            dve.wait_ge(sem("m2_o"), HJ)
            dve.tensor_scalar(hsq[:, :, :], hsq[:, :, :], 1.0 / P, EPS, ALU.mult, ALU.add).then_inc(sem("h_ms"), 1)
            dve.wait_ge(sem("h_root"), 1)
            dve.reciprocal(hrs[:, :, :], hrs[:, :, :]).then_inc(sem("h_rs"), 1)
            dve.wait_ge(sem("h_rs"), 1)
            for q in range(4):
                for t in range(NT):
                    o = mix2[:, t, q * GC:(q + 1) * GC].rearrange("p (h c) -> p h c", c=P)
                    dve.tensor_tensor(o, o, bcast(hrs[:, t, q * HPG:(q + 1) * HPG], 2, P), ALU.mult)\
                       .then_inc(sem("m2_mix"), 1)

        def mix2_ready(pe, q):
            pe.wait_ge(sem("m2_mix"), 2 * q + 2)

        def x0_ready(pe, q):
            pe.wait_ge(sem(f"x_in{q}"), 16)

        def gain_load(pool, ph, dst, name):
            pool.dma_start(dst[:, :], bcast(T[name][0], 0, P)).then_inc(sem(f"{ph}_gain"), 16)

        block = ctx.enter_context(nc.Block())

        @block.sync
        def _(sp):
            setup_sp(sp)
            in1_load(sp)
            m1_load(sp)
            back_load(sp, "out1", T["w_out"][0], CPG)
            up_load(sp, "up1", T["w_up"][0])
            back_load(sp, "down1", T["w_down"][0], DCH)
            m2_load(sp)
            back_load(sp, "out2", T["hgrn_w_out_2"][0], CPG)
            up_load(sp, "up2", T["ffn_w_in_2"][0])
            back_load(sp, "down2", T["ffn_w_out_2"][0], DCH)
            for q in range(4):
                c = slice(q * GC, (q + 1) * GC)
                sp.wait_ge(sem("down2_x"), 2 * q + 2)
                sp.dma_start(T["out"][0][:, c].rearrange("(n p) c -> p n c", p=P), x[:, :, c]).then_inc(sem("out"), 16)
            sp.wait_ge(sem("out"), 64)

        @block.gpsimd
        def _(pool):
            setup_pool(pool)
            pool.wait_ge(sem("m1_o"), UNITS)
            gain_load(pool, "out1", gbo1, "post_mix_norm")
            up_pool(pool, "up1")
            pool.wait_ge(chunk_used, cb["down1"])
            gain_load(pool, "down1", gbd, "post_ffn_norm")
            pool.wait_ge(chunk_used, cb["in2"])
            pool.dma_start(gnb[:, :], bcast(T["hgrn_gnorm_2"][0], 0, P)).then_inc(sem("m2_gn"), 16)
            pool.dma_start(lmask[:, :, :], T["lmask"]).then_inc(sem("m2_gn"), 16)
            gain_load(pool, "out2", gbo2, "norm_post_mix_2")
            up_pool(pool, "up2")
            pool.wait_ge(chunk_used, cb["down2"])
            gain_load(pool, "down2", gbd, "norm_post_ffn_2")

        @block.tensor
        def _(pe):
            setup_pe(pe)
            pre_pe(pe, "in1", x, x0_ready)
            in1_pe(pe)
            m1_pe(pe)
            pre_pe(pe, "out1", mix1, mix1_ready)
            back_pe(pe, "out1", ahi, alo, CPG, sem("pre_lo"), lo_ready("out1", KT - 1))
            pre_pe(pe, "up1", x, x_ready("out1"))
            up_pe(pe, "up1")
            back_pe(pe, "down1", hhi, hlo, DCH, sem("up1_hid"), FG, FG + 1)
            pre_pe(pe, "in2", x, x_ready("down1"))
            m2_pe(pe)
            pre_pe(pe, "out2", mix2, mix2_ready)
            back_pe(pe, "out2", ahi, alo, CPG, sem("pre_lo"), lo_ready("out2", KT - 1))
            pre_pe(pe, "up2", x, x_ready("out2"))
            up_pe(pe, "up2")
            back_pe(pe, "down2", hhi, hlo, DCH, sem("up2_hid"), FG, FG + 1)

        @block.scalar
        def _(act):
            setup_act(act)
            in1_act(act)
            m1_act(act)
            pre_act(act, "out1", None)
            back_act(act, "out1", 0, CPG)
            pre_act(act, "up1", 1)
            up_act(act, "up1", 0, sem("out1_x"), 8)
            back_act(act, "down1", 1, DCH)
            pre_act(act, "in2", 2)
            m2_act(act)
            pre_act(act, "out2", None)
            back_act(act, "out2", 2, CPG)
            pre_act(act, "up2", 3)
            up_act(act, "up2", 1, sem("out2_x"), 8)
            back_act(act, "down2", 3, DCH)

        @block.vector
        def _(dve):
            setup_dve(dve)
            in1_dve(dve)
            m1_dve(dve)
            pre_dve(dve, "out1", None)
            back_dve(dve, "out1", 0, CPG, gbo1)
            pre_dve(dve, "up1", 1)
            up_dve(dve, "up1", 0)
            back_dve(dve, "down1", 1, DCH, gbd)
            pre_dve(dve, "in2", 2)
            m2_dve(dve)
            pre_dve(dve, "out2", None)
            back_dve(dve, "out2", 2, CPG, gbo2)
            pre_dve(dve, "up2", 3)
            up_dve(dve, "up2", 1)
            back_dve(dve, "down2", 3, DCH, gbd)


_INS = ["x", "pre_mix_norm", "w_in", "lambda_q1", "lambda_k1", "lambda_q2", "lambda_k2", "diff_subln", "cmp_pos_k",
        "cmp_pos_v", "cmp_k_w1", "cmp_k_w2", "cmp_v_w1", "cmp_v_w2", "rel_bias", "w_out", "post_mix_norm",
        "pre_ffn_norm", "w_up", "conv_w", "conv_b", "w_down", "post_ffn_norm", "hgrn_w_in_2", "hgrn_w_out_2",
        "hgrn_gnorm_2", "ffn_w_in_2", "ffn_w_conv_2", "ffn_w_out_2", "norm_pre_mix_2", "norm_post_mix_2",
        "norm_pre_ffn_2", "norm_post_ffn_2"]


def _constants():
    import numpy as np
    delta = S - 1 - np.arange(TOEP)
    n = np.maximum(delta, 0)
    exact = N_BUCKETS // 2
    large = exact + (np.log(np.maximum(n, 1) / exact) / math.log(128 / exact) * (N_BUCKETS - exact)).astype(np.int32)
    bucket = np.where(n < exact, n, np.minimum(large, N_BUCKETS - 1))
    row = np.where(delta < 0, N_BUCKETS, bucket)
    onehot = (np.arange(N_BUCKETS + 1)[:, None] == row[None, :]).astype(np.float32)
    tok = np.arange(NT)[None, :, None] * P + np.arange(P)[:, None, None]
    seen = (np.arange(NC_)[None, None, :] * CMP_STRIDE + CMP_L - 1 <= tok).astype(np.float32)
    cmask = np.stack([seen, (1 - seen) * np.float32(NEG)], axis=1).astype(np.float32)
    s_ = (np.arange(P) % 32)[:, None, None]
    t_ = np.arange(32)[None, None, :]
    h = 2 ** np.arange(5)[None, :, None]
    m = (s_ // (2 * h) == t_ // (2 * h)) & (s_ // h != t_ // h)
    lmask = np.concatenate([m, s_ == t_], axis=1).astype(np.float32)
    return {"onehot": onehot, "cmask": np.ascontiguousarray(cmask), "lmask": np.ascontiguousarray(lmask)}


def kernel(**inputs):
    import numpy as _np
    import concourse.bacc as _bacc
    from concourse.bass_utils import run_bass_kernel_spmd as _run

    nc = _bacc.Bacc("TRN2", target_bir_lowering=False, num_devices=1)
    arrays, args = {}, {}
    for name in _INS:
        a = _np.ascontiguousarray(inputs[name])
        arrays[f"in_{name}_dram"] = a
        args[name] = nc.dram_tensor(f"in_{name}_dram", a.shape, mybir.dt.from_np(a.dtype), kind="ExternalInput").ap()
    for name, a in _constants().items():
        arrays[f"const_{name}_dram"] = a
        args[name] = nc.dram_tensor(f"const_{name}_dram", a.shape, mybir.dt.from_np(a.dtype), kind="ExternalInput").ap()
    args["scratch"] = nc.dram_tensor("scratch_dram", (16, P, TOEP), F32).ap()
    args["out"] = nc.dram_tensor("out_0_dram", (1, S, D), F32, kind="ExternalOutput").ap()
    bass_two_blocks(nc, args)
    r = _run(nc, [arrays], core_ids=[0])
    return r.results[0]["out_0_dram"]
```

```python
import math
from contextlib import ExitStack

import concourse.bass as bass
from concourse import mybir

ALU = mybir.AluOpType
ACT = mybir.ActivationFunctionType
F32 = mybir.dt.float32
F32R = mybir.dt.float32r
U8 = mybir.dt.uint8
AX = mybir.AxisListType

P = 128
S = 256
NT = S // P
D = 2048
KT = D // P
GC = 512
CK = 2
RING = 4
CPG = KT // CK
F = 5632
FT = F // P
DCH = FT // CK
NG = D // GC
FG = F // GC
EPS = 1e-6
NEG = -1e30
TINY = 1e-30

DIFF_H, NSA_H, NSA_KV = 8, 8, 2
NSA_GROUP = NSA_H // NSA_KV
DV, KC, VC, KS, VS, KW, VW = 2048, 4096, 4352, 4608, 4864, 5120, 5376
G0 = 5632
NGATE = 24
IN1 = G0 // GC
CMP_L, CMP_STRIDE, HID = 32, 16, 256
NC_ = (S - CMP_L) // CMP_STRIDE + 1
NCG = NSA_KV * NC_
CMP_LPC = CK * GC // HID
CMP_CH = CMP_L // CMP_LPC
LAM_INIT = 0.8 - 0.6 * math.exp(-0.3 * 0)
TOEP = 3 * P - 1
N_BUCKETS = 32

HPG = GC // P
HJ = D // GC
HGRP = 5
HCH = HGRP * CPG
N_LEV = 8
N_STEP = N_LEV + 1

TURN = ([KC, KC + P, VC, VC + P] + [P * j for j in range(16)] + [3072 + P * j for j in range(8)]
        + [KS, KS + P, KW, KW + P])
T_KC, T_VC, T_DQ, T_DK, T_NQ, T_KS, T_KW = 0, 2, 4, 12, 20, 28, 30


def bass_two_blocks(nc, T):
    with ExitStack() as ctx:
        def sb(name, shape, dt=F32, where=ctx):
            return where.enter_context(nc.sbuf_tensor(name, shape, dt))

        made = {}

        def sem(name):
            if name not in made:
                made[name] = ctx.enter_context(nc.semaphore(name))
            return made[name]

        raw = sb("raw", [P, RING, CK * GC])
        whi = sb("whi", [P, RING, CK * GC], F32R)
        wlo = sb("wlo", [P, RING, CK * GC], F32R)
        x = sb("x", [P, NT, D])
        ident = sb("ident", [P, P])
        gains = sb("gains", [P, 4, KT])
        taps = sb("taps", [P, 2, 4, 2 * FT])
        rstd = sb("rstd", [P, 4, NT])
        prs = sb("prs", [P, 4, NT])
        prime = sb("prime", [P, 1])
        psq = sb("psq", [P, 4, NT, NG])

        with ExitStack() as r:
            ybuf = sb("ybuf", [P, NT, D], where=r)
            hhi = sb("hhi", [P, FT, S], F32R, r)
            hlo = sb("hlo", [P, FT, S], F32R, r)
        with ExitStack() as r:
            utok = [sb(f"utok{j}", [P, NT, GC], where=r) for j in range(2)]
            cvg = sb("cvg", [P, 4, S], where=r)
            cvu = sb("cvu", [P, 4, S], where=r)
        with ExitStack() as r:
            sqj = sb("sqj", [P, D], where=r)
        with ExitStack() as r:
            ptok = sb("ptok", [P, NT, G0], where=r)
            qkT = sb("qkT", [P, 32, S], where=r)
            bias = sb("bias", [P, 16, S], where=r)
            wg = sb("wg", [P, KT, NGATE], where=r)
            wghl = sb("wghl", [P, KT, 2, NGATE], F32R, r)
            gsum = sb("gsum", [2 * NGATE, S], where=r)
            gfold = sb("gfold", [2 * NGATE, NGATE], where=r)
            cfold = sb("cfold", [2 * NCG, NCG], where=r)
            gate = sb("gate", [P, NT, NGATE], where=r)
            posT = sb("posT", [P, 2, CMP_L], where=r)
            w2 = sb("w2", [P, 2, 2, P], where=r)
            hidT = sb("hidT", [P, 2, 2, NCG], where=r)
            kcmpT = sb("kcmpT", [P, NCG], where=r)
            vcmp = sb("vcmp", [NC_, NSA_KV, P], where=r)
            cmask = sb("cmask", [P, 2, NT, NC_], where=r)
            sub = sb("sub", [P, P], where=r)
            lam4 = sb("lam4", [P, 4, 64], where=r)
            lamv = sb("lamv", [P, 8], where=r)
            pc = sb("pc", [P, NT, NSA_H, NC_], where=r)
            pcs = sb("pcs", [P, 4, NT, NSA_H], where=r)
            nmx = sb("nmx", [P, 32, 2], where=r)
            psm = sb("psm", [P, 32, 2], where=r)
            cof = sb("cof", [P, 32, 2], where=r)
            dsq = sb("dsq", [P, NT, DIFF_H], where=r)
            drs = sb("drs", [P, NT, DIFF_H], where=r)
        mix1 = ptok
        with ExitStack() as r:
            sb("hold0", [P, NT, G0], where=r)
            pst = sb("pst", [P, 8, P], where=r)
            tabaug = sb("tabaug", [N_BUCKETS + 1, 16], where=r)
            onehot = sb("onehot", [N_BUCKETS + 1, TOEP], where=r)
            toep = sb("toep", [16, TOEP], where=r)
        with ExitStack() as r:
            sb("hold1", [P, NT, G0], where=r)
            gbo1 = sb("gbo1", [P, D], where=r)
        with ExitStack() as r:
            mix2 = sb("mix2", [P, NT, D], where=r)
            gbo2 = sb("gbo2", [P, D], where=r)
            stg = sb("stg", [P, 3, NT, GC], where=r)
            sgm = sb("sgm", [P, NT, GC], where=r)
            qT = sb("qT", [P, HPG, S], where=r)
            kf = sb("kf", [P, HPG, S], where=r)
            kb = sb("kb", [P, HPG, S], where=r)
            pf = sb("pf", [P, HPG, S], where=r)
            sf = sb("sf", [P, HPG, S], where=r)
            ib = sb("ib", [P, HPG, S], where=r)
            eb = sb("eb", [P, HPG, S], where=r)
            qd = [sb(f"qd{j}", [P, HPG, S], where=r) for j in range(2)]
            kd = [sb(f"kd{j}", [P, HPG, S], where=r) for j in range(2)]
            at = sb("at", [P, HPG, NT, S], where=r)
            ad = sb("ad", [P, HPG, NT, 32], where=r)
            vt = sb("vt", [P, NT, GC], where=r)
            gs = sb("gs", [P, NT, GC], where=r)
            hsq = sb("hsq", [P, NT, 16], where=r)
            hrs = sb("hrs", [P, NT, 16], where=r)
            lmask = sb("lmask", [P, 6, 32], where=r)
            lpick = sb("lpick", [P, HPG * NT, 32], where=r)
            gnb = sb("gnb", [P, P], where=r)
        sb("hold2", [P, NT * D + 2 * FT * S + 512])
        with ExitStack() as r:
            ahi = sb("ahi", [P, KT, S], F32R, r)
            alo = sb("alo", [P, KT, S], F32R, r)
        with ExitStack() as r:
            blk = sb("blk", [P, 2, CMP_L, NCG], where=r)
        with ExitStack() as r:
            scb = [sb(f"scb{j}", [P, 2, S], where=r) for j in range(2)]
            prb = [sb(f"prb{j}", [P, 2, S], where=r) for j in range(2)]
            pts = [sb(f"pts{j}", [P, 5 * P], where=r) for j in range(2)]
            blkhl = sb("blkhl", [P, 2, CMP_L, 2, NCG], F32R, r)
            csum = sb("csum", [2 * NCG, 2, HID], where=r)
        with ExitStack() as r:
            gbd = sb("gbd", [P, D], where=r)

        acc = [ctx.enter_context(nc.psum_tensor(f"acc{i}", [P, NT, GC], F32)) for i in range(2)]
        tp = [ctx.enter_context(nc.psum_tensor(f"tp{i}", [P, 4, S], F32)) for i in range(2)]

        landed = [sem(f"landed{i}") for i in range(RING)]
        hi_done, lo_done, chunk_used = sem("hi_done"), sem("lo_done"), sem("chunk_used")
        group_free = sem("group_free")

        cb, gb = {}, {}
        n = g = 0
        for name, chunks, groups in (("in1", IN1 * CPG, IN1), ("cmp", 2 * CMP_CH, 0), ("out1", NG * CPG, NG),
                                     ("up1", 2 * FG * CPG, 2 * FG), ("down1", NG * DCH, NG),
                                     ("in2", HJ * HCH, HJ * HGRP), ("out2", NG * CPG, NG),
                                     ("up2", 2 * FG * CPG, 2 * FG), ("down2", NG * DCH, NG)):
            cb[name], gb[name] = n, g
            assert n % RING == 0
            n += chunks
            g += groups

        def load(sp, n, s, src, kk=CK):
            dst = raw[:, s, :].rearrange("p (k c) -> p k c", k=kk)
            if not (isinstance(n, int) and n < RING):
                sp.wait_ge(lo_done, n - RING + 1)
            sp.dma_start(dst, src).then_inc(landed[s], 16)

        def split_hi(act, n, s, turn):
            act.wait_ge(landed[s], turn)
            if not (isinstance(n, int) and n < RING):
                act.wait_ge(chunk_used, n - RING + 1)
            act.activation(whi[:, s, :], raw[:, s, :], ACT.Copy).then_inc(hi_done, 1)

        def split_lo(dve, n, s):
            dve.wait_ge(hi_done, n + 1)
            dve.tensor_tensor(wlo[:, s, :], raw[:, s, :], whi[:, s, :].bitcast(F32),
                              ALU.subtract).then_inc(lo_done, 1)

        def products(pe, n, s, out, xhi, xlo, k0, nk, ready=None):
            pe.wait_ge(lo_done, n + 1)
            for k in range(CK):
                kt = k0 + k
                if ready:
                    pe.wait_ge(sem("pre_lo"), lo_ready(ready, kt))
                c = slice(k * GC, (k + 1) * GC)
                for t in range(NT):
                    xh, xl = xhi[:, kt, t * P:(t + 1) * P], xlo[:, kt, t * P:(t + 1) * P]
                    pe.matmul(out[:, t, :], xh, whi[:, s, c], start=(kt == 0), stop=False)
                    pe.matmul(out[:, t, :], xh, wlo[:, s, c], start=False, stop=False)
                    mm = pe.matmul(out[:, t, :], xl, whi[:, s, c], start=False, stop=(kt == nk - 1))
            mm.then_inc(chunk_used, 1)

        def group(pe, g):
            if not (isinstance(g, int) and g < 2):
                pe.wait_ge(group_free, g - 1)

        def s_hi(act, ph, i, per, c):
            n = cb[ph] + c + i * per
            split_hi(act, n, c % RING, 16 * (cb[ph] // RING + c // RING + 1) + i * (16 * (per // RING)))

        def s_lo(dve, ph, i, per, c):
            split_lo(dve, cb[ph] + c + i * per, c % RING)

        def s_load(sp, ph, i, per, c, src, kk=CK):
            load(sp, cb[ph] + c + i * per, c % RING, src, kk)

        def w_tile(w, k0, col):
            return w[k0 * P:(k0 + CK) * P, bass.ds(col, GC)].rearrange("(k p) c -> p k c", p=P)

        PRE = ("in1", "out1", "up1", "in2", "out2", "up2")

        def lo_ready(ph, kt):
            return KT * PRE.index(ph) + kt + 1

        LEAD = 3

        def pre_pe(pe, ph, q, src, ready):
            ready(pe, q)
            if q >= 2:
                pe.wait_ge(sem("pre_lo"), lo_ready(ph, 4 * q - 5))
            for k in range(4):
                for t in range(NT):
                    c = (4 * q + k) * P
                    mm = pe.transpose(tp[q % 2][:, k, t * P:(t + 1) * P], src[:, t, c:c + P], ident[:, :])
            mm.then_inc(sem("pre_turned"), 1)

        def pre_act(act, ph, q, gain):
            act.wait_ge(sem("pre_turned"), 4 * PRE.index(ph) + q + 1)
            for k in range(4):
                kt = 4 * q + k
                act.activation(ahi[:, kt, :], tp[q % 2][:, k, :], ACT.Copy,
                               scale=1.0 if gain is None else gains[:, gain, kt:kt + 1])\
                   .then_inc(sem("pre_hi"), 1)

        def pre_dve(dve, ph, q, gain):
            for kt in range(4 * q, 4 * q + 4):
                dve.wait_ge(sem("pre_hi"), lo_ready(ph, kt | 1))
                turned, hi = tp[kt // 4 % 2][:, kt % 4, :], ahi[:, kt, :].bitcast(F32)
                if gain is None:
                    i = dve.tensor_tensor(alo[:, kt, :], turned, hi, ALU.subtract)
                else:
                    i = dve.scalar_tensor_tensor(out=alo[:, kt, :], in0=turned, scalar=gains[:, gain, kt:kt + 1],
                                                 in1=hi, op0=ALU.mult, op1=ALU.subtract)
                i.then_inc(sem("pre_lo"), 1)

        def lead_pe(pe, ph, c, src, ready):
            for q in {0: (0, 1), 2: (2,), 4: (3,)}.get(c, ()):
                pre_pe(pe, ph, q, src, ready)

        def lead_act(act, ph, c, gain):
            for q in {3: (0, 1), 5: (2,), 7: (3,)}.get(c, ()):
                pre_act(act, ph, q, gain)

        def lead_dve(dve, ph, c, gain, source):
            if c == 3:
                source(0)
                source(1)
                pre_dve(dve, ph, 0, gain)
                source(2)
                pre_dve(dve, ph, 1, gain)
            if c == 4:
                source(3)
            if c == 5:
                pre_dve(dve, ph, 2, gain)
            if c == 7:
                pre_dve(dve, ph, 3, gain)

        def sumsq_act(act, ph, k, x_sem, x_count):
            act.wait_ge(x_sem, x_count)
            for t in range(NT):
                if t:
                    act.wait_ge(sem(f"{ph}_sq"), 1)
                act.activation(sqj[:, :], x[:, t, :], ACT.Square,
                               accum_out=rstd[:, k, t:t + 1]).then_inc(sem(f"{ph}_sq"), 1)
            act.wait_ge(sem(f"{ph}_ms"), 1)
            act.activation(rstd[:, k, :], rstd[:, k, :], ACT.Sqrt).then_inc(sem(f"{ph}_root"), 1)

        def sumsq_dve(dve, ph, k):
            dve.wait_ge(sem(f"{ph}_sq"), NT)
            dve.tensor_scalar(rstd[:, k, :], rstd[:, k, :], 1.0 / D, EPS, ALU.mult, ALU.add)\
               .then_inc(sem(f"{ph}_ms"), 1)
            dve.wait_ge(sem(f"{ph}_root"), 1)
            dve.reciprocal(rstd[:, k, :], rstd[:, k, :]).then_inc(sem(f"{ph}_rstd"), 1)

        def back_load(sp, ph, w, nch):
            with sp.Fori(0, 2) as i:
                for c in range(2 * nch):
                    s_load(sp, ph, i, 2 * nch, c, w_tile(w, CK * (c % nch), i * (2 * GC) + c // nch * GC))

        def back_pe(pe, ph, xhi, xlo, nch, ready=None, ready_count=None, last_count=None, src=None, src_ready=None):
            def body(i, first):
                for c in range(2 * nch):
                    if c % nch == 0:
                        group(pe, gb[ph] + c // nch + 2 * i)
                    if first:
                        lead_pe(pe, ph, c, src, src_ready)
                    if last_count and CK * c == 4 * (FG - 1):
                        pe.wait_ge(ready, last_count)
                    products(pe, cb[ph] + c + i * (2 * nch), c % RING, acc[(gb[ph] + c // nch) % 2],
                             xhi, xlo, CK * (c % nch), CK * nch, ph if first and c < nch else None)
            if src is None:
                pe.wait_ge(ready, ready_count)
                with pe.Fori(0, 2) as i:
                    body(i, False)
            else:
                body(0, True)
                body(1, False)

        def back_group_dve(dve, ph, i, gg, nch, gain_row):
            dve.wait_ge(sem(f"{ph}_gain"), 16)
            dve.wait_ge(chunk_used, cb[ph] + (gg + 1) * nch + i * (2 * nch))
            a = acc[(gb[ph] + gg) % 2]
            col = i * (2 * GC) + gg * GC
            for t in range(NT):
                dve.tensor_tensor(ybuf[:, t, bass.ds(col, GC)], a[:, t, :], gain_row[:, bass.ds(col, GC)],
                                  ALU.mult).then_inc(sem(f"{ph}_y"), 1)

        def back_group_act(act, ph, k, i, gg):
            act.wait_ge(sem(f"{ph}_y"), i * 4 + (2 * gg + 2))
            a = acc[(gb[ph] + gg) % 2]
            for t in range(NT):
                m = act.activation(a[:, t, :], a[:, t, :], ACT.Square,
                                   accum_out=psq[:, k, t, bass.ds(i * 2 + gg, 1)])
            m.then_inc(group_free, 1)

        def back_act(act, ph, k, nch, first_too=False, last=False):
            def body(i, first, ahead=LEAD):
                for c in range(LEAD, 2 * nch + ahead):
                    if first:
                        lead_act(act, ph, c, None)
                    s_hi(act, ph, i, 2 * nch, c)
                    if c == nch + 3:
                        back_group_act(act, ph, k, i, 0)
                back_group_act(act, ph, k, i, 1)
            if first_too:
                body(0, True)
                body(1, False)
            elif last:
                body(0, False)
                body(1, False, 0)
            else:
                with act.Fori(0, 2) as i:
                    body(i, False)
            act.wait_ge(sem(f"{ph}_pms"), 2)
            act.activation(prs[:, k, :], prs[:, k, :], ACT.Sqrt).then_inc(sem(f"{ph}_proot"), 1)

        def back_dve(dve, ph, k, nch, gain_row, source=None, last=False):
            def body(i, first, ahead=LEAD):
                for c in range(LEAD, 2 * nch + ahead):
                    if first:
                        lead_dve(dve, ph, c, None, source)
                    s_lo(dve, ph, i, 2 * nch, c)
                    if c == nch + 3:
                        back_group_dve(dve, ph, i, 0, nch, gain_row)
                back_group_dve(dve, ph, i, 1, nch, gain_row)
            if source:
                body(0, True)
                body(1, False)
            elif last:
                body(0, False)
                body(1, False, 0)
            else:
                with dve.Fori(0, 2) as i:
                    body(i, False)
            dve.wait_ge(group_free, gb[ph] + NG)
            dve.tensor_reduce(prs[:, k, :], psq[:, k, :, :], AX.X, ALU.add).then_inc(sem(f"{ph}_pms"), 1)
            dve.wait_ge(sem(f"{ph}_pms"), 1)
            dve.tensor_scalar(prs[:, k, :], prs[:, k, :], 1.0 / D, EPS, ALU.mult, ALU.add)\
               .then_inc(sem(f"{ph}_pms"), 1)
            dve.wait_ge(sem(f"{ph}_proot"), 1)
            dve.reciprocal(prs[:, k, :], prs[:, k, :]).then_inc(sem(f"{ph}_prs"), 1)
            dve.wait_ge(sem(f"{ph}_prs"), 1)

        def add_rows(dve, ph, k):
            def add(q):
                c = slice(q * GC, (q + 1) * GC)
                for t in range(NT):
                    dve.scalar_tensor_tensor(out=x[:, t, c], in0=ybuf[:, t, c], scalar=prs[:, k, t:t + 1],
                                             in1=x[:, t, c], op0=ALU.mult, op1=ALU.add)\
                       .then_inc(sem(f"{ph}_x"), 1)
            return add

        def x_ready(ph):
            def wait(e, q):
                e.wait_ge(sem(f"{ph}_x"), 2 * q + 2)
            return wait

        BODY = 2 * CPG

        def up_load(sp, ph, w):
            def body(i):
                for c in range(BODY):
                    s_load(sp, ph, i, BODY, c, w_tile(w, CK * (c % CPG), i * GC + c // CPG * F))
            with sp.Fori(0, FG) as i:
                body(i)

        def up_pe(pe, ph, src_ready):
            def turn(i, half):
                pe.wait_ge(group_free, gb[ph] + half + 1 + i * 2)
                for k in range(4):
                    for t in range(NT):
                        mm = pe.transpose(tp[half][:, k, t * P:(t + 1) * P], utok[half][:, t, k * P:(k + 1) * P],
                                          ident[:, :])
                mm.then_inc(sem(f"{ph}_uturned{half}"), 1)

            def body(i, first):
                for c in range(BODY):
                    if c % CPG == 0:
                        group(pe, gb[ph] + c // CPG + i * 2)
                    if first:
                        lead_pe(pe, ph, c, x, src_ready)
                    products(pe, cb[ph] + c + i * BODY, c % RING, acc[(gb[ph] + c // CPG) % 2], ahi, alo,
                             CK * (c % CPG), KT, ph if first and c < CPG else None)
                    if c == 1 and not first:
                        turn(i - 1, 1)
                    if c == CPG + 1:
                        turn(i, 0)
            body(0, True)
            with pe.Fori(1, FG) as i:
                body(i, False)
            turn(FG - 1, 1)

        def up_act(act, ph, b, x_sem, x_count):
            cv = (cvg, cvu)

            def evacuate(i, half):
                act.wait_ge(chunk_used, cb[ph] + CPG * (half + 1) + i * BODY)
                for t in range(NT):
                    m = act.activation(utok[half][:, t, :], acc[(gb[ph] + half) % 2][:, t, :], ACT.Copy,
                                       scale=rstd[:, 2 * b + 1, t:t + 1])
                m.then_inc(group_free, 1)

            def centre(i, half):
                act.wait_ge(sem(f"{ph}_uturned{half}"), i + 1)
                act.wait_ge(sem(f"{ph}_hid"), i + 1)
                for k in range(4):
                    ct = i * 4 + (half * FT + k)
                    act.activation(cv[half][:, k, :], tp[half][:, k, :], ACT.Identity,
                                   bias=taps[:, b, 3, bass.ds(ct, 1)],
                                   scale=taps[:, b, 2 - b, bass.ds(ct, 1)]).then_inc(sem(f"{ph}_centre{half}"), 1)

            def nonlinear(i):
                act.wait_ge(sem(f"{ph}_conv0"), i * 8 + 8)
                act.activation(cvg[:, :, :], cvg[:, :, :], ACT.Silu if b else ACT.Gelu_apprx_tanh)\
                   .then_inc(sem(f"{ph}_nl"), 1)

            def body(i, first):
                for c in range(LEAD if first else 0, BODY):
                    if first:
                        lead_act(act, ph, c, 2 * b + 1)
                    s_hi(act, ph, i, BODY, c)
                    if c == 0 and not first:
                        nonlinear(i - 1)
                    if c == 3 and not first:
                        evacuate(i - 1, 1)
                    if c == 7 and first:
                        sumsq_act(act, ph, 2 * b + 1, x_sem, x_count)
                    if c == 5 and not first:
                        centre(i - 1, 1)
                    if c == CPG + 3:
                        if first:
                            act.wait_ge(sem(f"{ph}_rstd"), 1)
                        evacuate(i, 0)
                    if c == CPG + 5:
                        centre(i, 0)
            body(0, True)
            with act.Fori(1, FG) as i:
                body(i, False)
            nonlinear(FG - 1)
            for c in range(LEAD):
                s_hi(act, f"down{b + 1}", 0, 0, c)
            evacuate(FG - 1, 1)
            centre(FG - 1, 1)

        def up_dve(dve, ph, b, source):
            cv = (cvg, cvu)

            def convolve(i, half):
                dve.wait_ge(sem(f"{ph}_centre{half}"), i * 4 + 4)
                for j, (tap, d) in enumerate((((1, 1), (0, 2)), ((0, 1), (2, -1)))[b]):
                    if j:
                        dve.wait_ge(sem(f"{ph}_conv{half}"), i * 8 + 4)
                    o = slice(d, S) if d > 0 else slice(0, S + d)
                    u = slice(0, S - d) if d > 0 else slice(-d, S)
                    for k in range(4):
                        ct = i * 4 + (half * FT + k)
                        dve.scalar_tensor_tensor(out=cv[half][:, k, o], in0=tp[half][:, k, u],
                                                 scalar=taps[:, b, tap, bass.ds(ct, 1)], in1=cv[half][:, k, o],
                                                 op0=ALU.mult, op1=ALU.add).then_inc(sem(f"{ph}_conv{half}"), 1)

            def body(i, first):
                for c in range(LEAD if first else 0, BODY):
                    if first:
                        lead_dve(dve, ph, c, 2 * b + 1, source)
                    s_lo(dve, ph, i, BODY, c)
                    if c == 7 and first:
                        sumsq_dve(dve, ph, 2 * b + 1)
                    if c == 6 and not first:
                        convolve(i - 1, 1)
                    if c == CPG + 6:
                        convolve(i, 0)
            body(0, True)
            with dve.Fori(1, FG) as i:
                body(i, False)
            for c in range(LEAD):
                s_lo(dve, f"down{b + 1}", 0, 0, c)
            convolve(FG - 1, 1)

        def up_pool(pool, ph):
            pool.memset(prime[:, :], 0.0).then_inc(sem(f"{ph}_hid"), 1)
            with pool.Fori(0, FG) as i:
                pool.wait_ge(sem(f"{ph}_nl"), i + 1)
                pool.wait_ge(sem(f"{ph}_conv1"), i * 8 + 8)
                pool.tensor_tensor(cvg[:, :, :], cvg[:, :, :], cvu[:, :, :], ALU.mult).then_inc(sem(f"{ph}_pr"), 1)
                pool.wait_ge(sem(f"{ph}_pr"), i + 1)
                pool.tensor_copy(hhi[:, bass.ds(i * 4, 4), :], cvg[:, :, :]).then_inc(sem(f"{ph}_hh"), 1)
                pool.wait_ge(sem(f"{ph}_hh"), i + 1)
                pool.tensor_tensor(hlo[:, bass.ds(i * 4, 4), :], cvg[:, :, :],
                                   hhi[:, bass.ds(i * 4, 4), :].bitcast(F32), ALU.subtract)\
                    .then_inc(sem(f"{ph}_hid"), 1)

        def bcast(ap, at, n):
            a = [list(d) for d in ap.ap]
            return bass.AP(tensor=ap.tensor, offset=ap.offset, ap=a[:at] + [[0, n]] + a[at:])

        def strided(ap, dims):
            return bass.AP(tensor=ap.tensor, offset=ap.offset, ap=[list(ap.ap[0])] + [list(d) for d in dims])

        par_in, mix_in = sem("par_in"), sem("mix_in")

        def x_load(sp, quarters):
            for q in quarters:
                c = slice(q * GC, (q + 1) * GC)
                sp.dma_start(x[:, :, c], T["x"][0][:, c].rearrange("(n p) c -> p n c", p=P)).then_inc(sem(f"x_in{q}"), 16)

        ROWS = [("pre_mix_norm", 0, 0), ("pre_ffn_norm", 0, KT), ("norm_pre_mix_2", 0, 2 * KT),
                ("norm_pre_ffn_2", 0, 3 * KT), ("cmp_pos_k", 0, 4 * KT), ("cmp_pos_v", 0, 4 * KT + CMP_L)]

        def rows_load(e, rows):
            for name, j, r in rows:
                src = T[name].rearrange("a (r c) -> (a r) c", c=P) if "norm" in name else T[name][0]
                e.dma_start(pst[r:r + src.shape[0], j, :], src).then_inc(sem("rows_in"), 16)

        def later_sp(sp):
            for j in range(3):
                sp.dma_start(pst[0:2 * FT, 1 + j, :], T["conv_w"][0, j].rearrange("(r c) -> r c", c=P)).then_inc(par_in, 16)
                sp.dma_start(pst[0:2 * FT, 5 + j, :], T["ffn_w_conv_2"][0, j].rearrange("(r c) -> r c", c=P)).then_inc(par_in, 16)
            sp.dma_start(pst[0:2 * FT, 4, :], T["conv_b"][0].rearrange("(r c) -> r c", c=P)).then_inc(par_in, 16)
            sp.dma_start(tabaug[0:N_BUCKETS, :], T["rel_bias"]).then_inc(par_in, 16)
            sp.dma_start(onehot[:, :], T["onehot"]).then_inc(par_in, 16)

        N_PAR = 9 * 16

        def setup_pool(pool):
            pool.memset(ident[:, :], 0.0).then_inc(sem("ident"), 1)
            pool.wait_ge(sem("ident"), 1)
            pool.memset(tabaug[N_BUCKETS:N_BUCKETS + 1, :], NEG).then_inc(sem("ident"), 1)
            pool.wait_ge(sem("ident"), 2)
            pool.affine_select(out=ident[:, :], in_=ident[:, :], compare_op=ALU.not_equal, fill=1.0, base=0,
                               pattern=[[-1, P]], channel_multiplier=1).then_inc(sem("ident"), 1)
            pool.dma_start(wg[:, :, :], T["w_in"][0][:, G0:G0 + NGATE].rearrange("(k p) c -> p k c", p=P)).then_inc(mix_in, 16)
            for a, name in enumerate(("cmp_k_w2", "cmp_v_w2")):
                pool.dma_start(w2[:, a, :, :], T[name][0].rearrange("(k p) c -> p k c", p=P)).then_inc(mix_in, 16)
            pool.dma_start(cmask[:, :, :, :], T["cmask"]).then_inc(mix_in, 16)
            pool.dma_start(sub[:, :], bcast(T["diff_subln"][0], 0, P)).then_inc(mix_in, 16)
            for j, name in enumerate(("lambda_q1", "lambda_k1", "lambda_q2", "lambda_k2")):
                pool.dma_start(lam4[:, j, :], bcast(T[name][0], 0, P)).then_inc(mix_in, 16)
            pool.wait_ge(sem("toep"), 1)
            pool.dma_start(T["scratch"], bass.AP(tensor=toep, offset=0, ap=[[TOEP, 16], [0, P], [1, TOEP]]))\
                .then_inc(sem("skew_out"), 16)
            pool.wait_ge(sem("skew_out"), 16)
            t = T["scratch"]
            pool.dma_start(bias[:, :, :], bass.AP(tensor=t.tensor, offset=t.offset + P - 1,
                                                  ap=[[TOEP - 1, P], [P * TOEP, 16], [1, S]]))\
                .then_inc(sem("bias_in"), 16)

        N_MIX = 9 * 16

        def setup_pe(pe):
            pe.wait_ge(sem("ident"), 3)
            pe.wait_ge(sem("rows_in"), len(ROWS) * 16)
            pe.transpose(acc[0][:, 0, 0:P], pst[:, 0, :], ident[:, :]).then_inc(sem("par_turned"), 1)

        def later_pe(pe):
            pe.wait_ge(par_in, N_PAR)
            for j in range(1, 8):
                mm = pe.transpose(tp[0][:, (j - 1) // 2, (j - 1) % 2 * P:(j - 1) % 2 * P + 2 * FT],
                                  pst[0:2 * FT, j, :], ident[0:2 * FT, 0:2 * FT])
            mm.then_inc(sem("par_turned"), 1)
            pe.matmul(tp[1][0:16, 0:2, :].rearrange("p k t -> p (k t)")[:, 0:TOEP], tabaug[:, :], onehot[:, :],
                      start=True, stop=True).then_inc(sem("toep_sum"), 1)

        def setup_dve(dve):
            dve.memset(taps[:, 1, 3, :], 0.0)
            dve.wait_ge(sem("ident"), 3)
            dve.tensor_tensor(gfold[:, :], ident[0:2 * NGATE, 0:NGATE], ident[0:2 * NGATE, NGATE:2 * NGATE], ALU.add)\
               .then_inc(sem("fold"), 1)
            dve.tensor_tensor(cfold[:, :], ident[0:2 * NCG, 0:NCG], ident[0:2 * NCG, NCG:2 * NCG], ALU.add)\
               .then_inc(sem("fold"), 1)
            dve.wait_ge(sem("par_turned"), 1)
            a = acc[0]
            dve.tensor_copy(gains[:, :, :].rearrange("p a k -> p (a k)"), a[:, 0, 0:4 * KT]).then_inc(sem("par_ok"), 1)
            dve.tensor_copy(posT[:, :, :].rearrange("p a k -> p (a k)"), a[:, 0, 4 * KT:P]).then_inc(sem("par_ok"), 1)

        def later_dve(dve):
            dve.wait_ge(sem("par_turned"), 2)
            for j in range(1, 8):
                b, tap = (0, j - 1) if j < 5 else (1, j - 5)
                dve.tensor_copy(taps[:, b, tap, :],
                                tp[0][:, (j - 1) // 2, (j - 1) % 2 * P:(j - 1) % 2 * P + 2 * FT]).then_inc(sem("par_ok"), 1)

        def in1_load(sp):
            w = T["w_in"][0]

            def body(i, first=False):
                for c in range(BODY):
                    s_load(sp, "in1", i, BODY, c, w_tile(w, CK * (c % CPG), i * (2 * GC) + c // CPG * GC))
                    if first and c < 2:
                        x_load(sp, (2 + c,))
                    if first and c == RING - 1:
                        later_sp(sp)
            body(0, True)
            with sp.Fori(1, IN1 // 2) as i:
                body(i)
            for c in range(CPG):
                s_load(sp, "in1", IN1 // 2, BODY, c, w_tile(w, CK * c, (IN1 - 1) * GC))

        def in1_pe(pe):
            pe.wait_ge(sem("par_ok"), 2)

            def half(i, h, ready=None):
                group(pe, h + i * 2)
                for c in range(CPG):
                    if ready:
                        lead_pe(pe, "in1", c, x, x0_ready)
                    cc = h * CPG + c
                    products(pe, cb["in1"] + cc + i * BODY, cc % RING, acc[h], ahi, alo, CK * c, KT, ready)
            half(0, 0, "in1")
            later_pe(pe)
            half(0, 1)
            with pe.Fori(1, IN1 // 2) as i:
                half(i, 0)
                half(i, 1)
            group(pe, IN1 - 1)
            for c in range(CPG):
                products(pe, cb["in1"] + c + IN1 // 2 * BODY, c % RING, acc[0], ahi, alo, CK * c, KT)
                if c == 4:
                    gate_sums(pe)
            pe.wait_ge(sem("gate_sb"), 1)
            for t in range(NT):
                mm = pe.matmul(tp[0][:, 2 * t, 0:NGATE], gsum[:, t * P:(t + 1) * P], gfold[:, :], start=True, stop=True)
            mm.then_inc(sem("gate_fold"), 1)

        def gate_sums(pe):
            pe.wait_ge(sem("wg_lo"), 1)
            pe.wait_ge(sem("fold"), 2)
            pe.wait_ge(sem("par_ok"), 9)
            for kt in range(KT):
                both, hi = wghl[:, kt, :, :].rearrange("p a c -> p (a c)"), wghl[:, kt, 0, :]
                one = (tp[0][0:2 * NGATE, 0, :], both, ahi[:, kt, :])
                two = (tp[0][0:NGATE, 0, :], hi, alo[:, kt, :])
                for j, (o, w, a) in enumerate((two, one) if kt == KT - 1 else (one, two)):
                    mm = pe.matmul(o, w, a, start=(kt == 0 and j == 0), stop=(kt == KT - 1 and j == 1))
            mm.then_inc(sem("gate_sum"), 1)

        def in1_act(act):
            s_hi(act, "in1", 0, 0, 0)
            act.wait_ge(sem("par_ok"), 1)
            for q in range(2):
                pre_act(act, "in1", q, 0)
            for c in range(1, LEAD):
                s_hi(act, "in1", 0, 0, c)

            def evacuate(i, h):
                act.wait_ge(chunk_used, cb["in1"] + CPG * (h + 1) + i * BODY)
                for t in range(NT):
                    m = act.activation(ptok[:, t, bass.ds(i * (2 * GC) + h * GC, GC)], acc[h][:, t, :], ACT.Copy,
                                       scale=rstd[:, 0, t:t + 1])
                m.then_inc(group_free, 1)

            def body(i, first):
                for c in range(LEAD if first else 0, BODY):
                    if first and c > LEAD:
                        lead_act(act, "in1", c, 0)
                    s_hi(act, "in1", i, BODY, c)
                    if first and c == 7:
                        sumsq_act(act, "in1", 0, sem("x_in3"), 16)
                        act.wait_ge(mix_in, N_MIX)
                        act.activation(wghl[:, :, 0, :], wg[:, :, :], ACT.Copy).then_inc(sem("wg_hi"), 1)
                        act.wait_ge(sem("in1_rstd"), 1)
                    if not first and c == 3:
                        evacuate(i - 1, 1)
                    if c == CPG + 3:
                        evacuate(i, 0)
                    if first and c == CPG + 3:
                        act.wait_ge(sem("toep_sum"), 1)
                        act.activation(toep[:, :], tp[1][0:16, 0:2, :].rearrange("p k t -> p (k t)")[:, 0:TOEP],
                                       ACT.Copy).then_inc(sem("toep"), 1)
            body(0, True)
            with act.Fori(1, IN1 // 2) as i:
                body(i, False)
            for c in range(CPG):
                s_hi(act, "in1", IN1 // 2, BODY, c)
                if c == 3:
                    evacuate(IN1 // 2 - 1, 1)
            act.wait_ge(sem("gate_sum"), 1)
            act.activation(gsum[:, :], tp[0][0:2 * NGATE, 0, :], ACT.Copy).then_inc(sem("gate_sb"), 1)
            evacuate(IN1 // 2, 0)
            act.wait_ge(sem("gate_fold"), 1)
            for t in range(NT):
                act.activation(gate[:, t, :], tp[0][:, 2 * t, 0:NGATE], ACT.Sigmoid, scale=rstd[:, 0, t:t + 1])\
                   .then_inc(sem("gate"), 1)
            act.wait_ge(sem("lam_sum"), 2)
            act.activation(lamv[:, 2:4], lamv[:, 0:2], ACT.Exp).then_inc(sem("lam_exp"), 1)

        def in1_dve(dve):
            s_lo(dve, "in1", 0, 0, 0)
            for q in range(2):
                pre_dve(dve, "in1", q, 0)
                s_lo(dve, "in1", 0, 0, q + 1)

            def body(i, first):
                for c in range(LEAD if first else 0, BODY):
                    if first and c > LEAD:
                        lead_dve(dve, "in1", c, 0, lambda q: None)
                    s_lo(dve, "in1", i, BODY, c)
                    if first and c == 7:
                        sumsq_dve(dve, "in1", 0)
                        dve.wait_ge(sem("wg_hi"), 1)
                        dve.tensor_tensor(wghl[:, :, 1, :], wg[:, :, :], wghl[:, :, 0, :].bitcast(F32), ALU.subtract)\
                           .then_inc(sem("wg_lo"), 1)
                        dve.wait_ge(mix_in, N_MIX)
                        dve.tensor_tensor(lam4[:, 0:3:2, :], lam4[:, 0:3:2, :], lam4[:, 1:4:2, :], ALU.mult)\
                           .then_inc(sem("lam_sum"), 1)
                        dve.wait_ge(sem("lam_sum"), 1)
                        dve.tensor_reduce(lamv[:, 0:2], lam4[:, 0:3:2, :], AX.X, ALU.add).then_inc(sem("lam_sum"), 1)
                        dve.tensor_scalar(sub[:, :], sub[:, :], 1.0 - LAM_INIT, None, ALU.mult).then_inc(sem("sub"), 1)
                    if first and c == CPG + 3:
                        later_dve(dve)
            body(0, True)
            with dve.Fori(1, IN1 // 2) as i:
                body(i, False)
            for c in range(CPG):
                s_lo(dve, "in1", IN1 // 2, BODY, c)
            dve.wait_ge(sem("lam_exp"), 1)
            dve.scalar_tensor_tensor(out=lamv[:, 4:5], in0=lamv[:, 3:4], scalar=-LAM_INIT, in1=lamv[:, 2:3],
                                     op0=ALU.add, op1=ALU.subtract).then_inc(sem("nlam"), 1)

        UNITS = 2 * (DIFF_H + NSA_H)

        def unit(u):
            return (u % 16) // 2, u % 2, P * (u % 2 + 1)

        cps = [tp[a][:, 2:4, :].rearrange("p k t -> p (k t)") for a in range(2)]

        def unit_out(u):
            c = (3 if u < 16 else 7) * P
            return tp[u % 2][:, :, :].rearrange("p k t -> p (k t)")[:, c:c + P]

        CA = "cmp"

        def m1_load(sp):
            for a, name in enumerate(("cmp_k_w1", "cmp_v_w1")):
                for c in range(CMP_CH):
                    src = T[name][0][c * CMP_LPC * P:(c + 1) * CMP_LPC * P, :].rearrange("(k p) c -> p k c", p=P)
                    s_load(sp, CA, 0, 0, a * CMP_CH + c, src, CMP_LPC)

        def m1_pe(pe):
            pe.wait_ge(group_free, IN1)
            for b in range(8):
                if b == 1:
                    pe.wait_ge(sem("gate"), NT)
                if b >= 2:
                    pe.wait_ge(sem(f"m1_turn_read{b % 2}"), b // 2)
                for k in range(4):
                    for t in range(NT):
                        c = TURN[4 * b + k]
                        mm = pe.transpose(tp[(b + 1) % 2][:, k, t * P:(t + 1) * P], ptok[:, t, c:c + P], ident[:, :])
                mm.then_inc(sem("m1_turned"), 1)
            pe.wait_ge(sem("m1_turn_read0"), 4)
            pe.wait_ge(sem("m1_turn_read1"), 4)

            def hidden(c):
                a = c // CMP_CH
                if c % CMP_CH == 0:
                    pe.wait_ge(sem("blk_lo"), a + 1)
                n = cb[CA] + c
                pe.wait_ge(lo_done, n + 1)
                for k in range(CMP_LPC):
                    l = c % CMP_CH * CMP_LPC + k
                    cc = slice(k * HID, (k + 1) * HID)
                    both, hi = blkhl[:, a, l, :, :].rearrange("p a c -> p (a c)"), blkhl[:, a, l, 0, :]
                    one = (cps[a][0:2 * NCG, 0:HID], both, whi[:, n % RING, cc])
                    two = (cps[a][0:NCG, 0:HID], hi, wlo[:, n % RING, cc])
                    for j, (o, b_, w) in enumerate((two, one) if l == CMP_L - 1 else (one, two)):
                        mm = pe.matmul(o, b_, w, start=(l == 0 and j == 0), stop=(l == CMP_L - 1 and j == 1))
                mm.then_inc(chunk_used, 1)

            def compress(u):
                if u < CMP_CH:
                    hidden(2 * u)
                    hidden(2 * u + 1)
                if u == 9:
                    pe.wait_ge(sem("cmp_sum"), 2)
                    for a in range(2):
                        for ht in range(2):
                            mm = pe.matmul(cps[a][:, ht * NCG:(ht + 1) * NCG], csum[:, a, ht * P:(ht + 1) * P],
                                           cfold[:, :], start=True, stop=True)
                    mm.then_inc(sem("cmp_fold"), 1)
                if u == 11:
                    pe.wait_ge(sem("cmp_hid"), 2)
                    for ht in range(2):
                        pe.matmul(cps[0][:, 2 * P:2 * P + NCG], w2[:, 0, ht, :], hidT[:, 0, ht, :],
                                  start=(ht == 0), stop=(ht == 1))
                    for g in range(NSA_KV):
                        for ht in range(2):
                            mm = pe.matmul(cps[0][0:NC_, g * P:(g + 1) * P], hidT[:, 1, ht, g * NC_:(g + 1) * NC_],
                                           w2[:, 1, ht, :], start=(ht == 0), stop=(ht == 1))
                    mm.then_inc(sem("cmp_kv"), 1)
                if u in (13, 14):
                    qt = u - 13
                    pe.wait_ge(sem("cmp_kv_ok"), 2)
                    for h in range(NSA_H):
                        g, c = h // NSA_GROUP, (qt * NSA_H + h) * NC_
                        mm = pe.matmul(cps[1][:, c:c + NC_], qkT[:, T_NQ + h, qt * P:(qt + 1) * P],
                                       kcmpT[:, g * NC_:(g + 1) * NC_], start=True, stop=True)
                    mm.then_inc(sem("cmp_sc"), 1)

            def scores(u):
                h, qt, nk = unit(u)
                if u >= 2:
                    pe.wait_ge(sem("m1_sb"), u - 1)
                if u < 16:
                    for m in range(2):
                        r = slice(64 * m, 64 * m + 64)
                        mm = pe.matmul(acc[u % 2][:, m, 0:nk], qkT[r, T_DQ + h, qt * P:(qt + 1) * P],
                                       qkT[r, T_DK + h, 0:nk], start=True, stop=True)
                else:
                    keys = strided(qkT[:, T_KS + h // NSA_GROUP, 0:1], [[(T_KW - T_KS) * S, 2], [1, nk]])
                    mm = pe.matmul(acc[u % 2][:, 0, 0:2 * nk].rearrange("p (m k) -> p m k", m=2),
                                   qkT[:, T_NQ + h, qt * P:(qt + 1) * P], keys, start=True, stop=True)
                mm.then_inc(sem("m1_sc"), 1)

            def flat(u):
                return tp[u % 2][:, :, :].rearrange("p k t -> p (k t)")

            def turn(u):
                h, qt, nk = unit(u)
                if u >= 2:
                    pe.wait_ge(sem("m1_o"), u - 1)
                pe.wait_ge(sem("m1_p"), u + 1)
                if u >= 16:
                    pe.wait_ge(sem("pc"), 1)
                for m in range(1 if u < 16 else 2):
                    for kt in range(nk // P):
                        c = m * nk + kt * P
                        mm = pe.transpose(flat(u)[:, c:c + P], prb[u % 2][:, m, kt * P:(kt + 1) * P], ident[:, :])
                if u >= 16:
                    mm = pe.transpose(flat(u)[0:NC_, 2 * nk:2 * nk + P], pc[:, qt, h, :], ident[:, :])
                mm.then_inc(sem("m1_turned"), 1)

            def weighted(u):
                h, qt, nk = unit(u)
                o = unit_out(u)
                pe.wait_ge(sem("m1_pt"), u + 1)
                t = pts[u % 2]
                if u < 16:
                    for kt in range(nk // P):
                        mm = pe.matmul(o, t[:, kt * P:(kt + 1) * P], ptok[:, kt, DV + h * P:DV + (h + 1) * P],
                                       start=(kt == 0), stop=(kt == nk // P - 1))
                else:
                    g = h // NSA_GROUP
                    for m, v in enumerate((VS, VW)):
                        for kt in range(nk // P):
                            c = m * nk + kt * P
                            pe.matmul(o, t[:, c:c + P], ptok[:, kt, v + g * P:v + (g + 1) * P],
                                      start=(m == 0 and kt == 0), stop=False)
                    mm = pe.matmul(o, t[0:NC_, 2 * nk:2 * nk + P], vcmp[:, g, :], start=False, stop=True)
                mm.then_inc(sem("m1_pv"), 1)

            for u in range(3):
                scores(u)
            for u in range(UNITS):
                compress(u)
                if u >= 1:
                    weighted(u - 1)
                if u + 3 < UNITS:
                    scores(u + 3)
                turn(u)
            weighted(UNITS - 1)

        def m1_act(act):
            act.wait_ge(sem("skew_out"), 16)
            for b in range(0, 8, 2):
                act.wait_ge(sem("m1_turned"), b + 1)
                act.activation(qkT[:, 4 * b:4 * b + 4, :], tp[1][:, :, :], ACT.Copy).then_inc(sem("m1_turn_read0"), 1)
            for a in range(2):
                act.wait_ge(sem("blk"), 4 * a + 4)
                act.activation(blkhl[:, a, :, 0, :], blk[:, a, :, :], ACT.Copy).then_inc(sem("blk_hi"), 1)
            s_hi(act, CA, 0, 0, 0)
            s_hi(act, CA, 0, 0, 1)

            def compress(u):
                if u == 7:
                    act.wait_ge(chunk_used, cb[CA] + 2 * CMP_CH)
                    for a in range(2):
                        act.activation(csum[:, a, :], cps[a][0:2 * NCG, 0:HID], ACT.Copy).then_inc(sem("cmp_sum"), 1)
                if u == 9:
                    act.wait_ge(sem("cmp_fold"), 1)
                    for a in range(2):
                        act.activation(hidT[:, a, :, :].rearrange("p h c -> p (h c)"), cps[a][:, 0:2 * NCG],
                                       ACT.Gelu_apprx_tanh).then_inc(sem("cmp_hid"), 1)
                if u == 11:
                    act.wait_ge(sem("cmp_kv"), 1)
                    act.activation(kcmpT[:, :], cps[0][:, 2 * P:2 * P + NCG], ACT.Copy).then_inc(sem("cmp_kv_ok"), 1)
                    act.activation(vcmp[:, :, :].rearrange("p g c -> p (g c)"), cps[0][0:NC_, 0:2 * P], ACT.Copy)\
                       .then_inc(sem("cmp_kv_ok"), 1)
                if 16 <= u < 16 + LEAD:
                    s_hi(act, "out1", 0, 0, u - 16)
                if u == 14:
                    act.wait_ge(sem("pc_sub"), 1)
                    act.activation(pc[:, :, :, :], pc[:, :, :, :], ACT.Exp).then_inc(sem("pc_exp"), 1)

            def flat(u):
                return tp[u % 2][:, :, :].rearrange("p k t -> p (k t)")

            def exps(u):
                h, qt, nk = unit(u)
                act.wait_ge(sem("m1_max"), u + 1)
                if u >= 2:
                    act.wait_ge(sem("m1_turned"), 8 + u - 1)
                for m in range(2):
                    act.activation(prb[u % 2][:, m, 0:nk], scb[u % 2][:, m, 0:nk], ACT.Exp,
                                   bias=nmx[:, u, m:m + 1], accum_out=psm[:, u, m:m + 1]).then_inc(sem("m1_e"), 1)

            def turned(u):
                h, qt, nk = unit(u)
                act.wait_ge(sem("m1_turned"), 8 + u + 1)
                if u >= 2:
                    act.wait_ge(sem("m1_pv"), u - 1)
                if u < 16:
                    m = act.activation(pts[u % 2][:, 0:nk], flat(u)[:, 0:nk], ACT.Copy)
                else:
                    act.activation(pts[u % 2][0:NC_, 2 * nk:2 * nk + P], flat(u)[0:NC_, 2 * nk:2 * nk + P], ACT.Copy)
                    m = act.activation(pts[u % 2][:, 0:2 * nk], flat(u)[:, 0:2 * nk], ACT.Copy)
                m.then_inc(sem("m1_pt"), 1)

            def outs(u):
                h, qt, nk = unit(u)
                o = unit_out(u)
                act.wait_ge(sem("m1_pv"), u + 1)
                c = (0 if u < 16 else DIFF_H * P) + h * P
                m = act.activation(mix1[:, qt, c:c + P], o, ACT.Copy)
                if u < 16:
                    m = act.activation(o, o, ACT.Square, accum_out=dsq[:, qt, h:h + 1])
                m.then_inc(sem("m1_o"), 1)

            exps(0)
            exps(1)
            for u in range(UNITS):
                if u < CMP_CH - 1:
                    s_hi(act, CA, 0, 0, 2 * u + 2)
                if u >= 1:
                    outs(u - 1)
                if u < CMP_CH - 1:
                    s_hi(act, CA, 0, 0, 2 * u + 3)
                turned(u)
                if u + 2 < UNITS:
                    exps(u + 2)
                compress(u)
                if u == 18:
                    act.wait_ge(sem("d_ms"), 1)
                    act.activation(drs[:, :, :], dsq[:, :, :], ACT.Sqrt).then_inc(sem("d_root"), 1)
            outs(UNITS - 1)

        def m1_dve(dve):
            dve.wait_ge(sem("skew_out"), 16)
            for b in range(8):
                if b % 2:
                    dve.wait_ge(sem("m1_turned"), b + 1)
                    dve.tensor_copy(qkT[:, 4 * b:4 * b + 4, :], tp[0][:, :, :]).then_inc(sem("m1_turn_read1"), 1)
                if b == 3:
                    dve.wait_ge(sem("m1_turn_read0"), 1)
                    for a in range(2):
                        for g in range(NSA_KV):
                            for lh in range(2):
                                l0 = lh * CMP_STRIDE
                                t = qkT[:, (T_KC, T_VC)[a] + g, l0:l0 + 1]
                                dve.tensor_tensor(
                                    blk[:, a, l0:l0 + CMP_STRIDE, g * NC_:(g + 1) * NC_],
                                    strided(t, [[1, CMP_STRIDE], [CMP_STRIDE, NC_]]),
                                    strided(posT[:, a, l0:l0 + 1], [[1, CMP_STRIDE], [0, NC_]]), ALU.add)\
                                   .then_inc(sem("blk"), 1)
            for a in range(2):
                dve.wait_ge(sem("blk_hi"), a + 1)
                dve.wait_ge(sem("blk"), 4 * a + 4)
                dve.tensor_tensor(blkhl[:, a, :, 1, :], blk[:, a, :, :], blkhl[:, a, :, 0, :].bitcast(F32),
                                  ALU.subtract).then_inc(sem("blk_lo"), 1)
            s_lo(dve, CA, 0, 0, 0)
            s_lo(dve, CA, 0, 0, 1)
            w_ = pc[:, :, :, :].rearrange("p n h c -> p (n h) c")
            st = [pcs[:, j, :, :].rearrange("p n h -> p (n h)") for j in range(4)]

            def wide(a):
                return bcast(a, 2, NC_)

            def compress(u):
                if 16 <= u < 16 + LEAD:
                    s_lo(dve, "out1", 0, 0, u - 16)
                if u == 14:
                    dve.wait_ge(sem("cmp_sc"), NT)
                    for qt in range(NT):
                        s_ = cps[1][:, qt * NSA_H * NC_:(qt + 1) * NSA_H * NC_].rearrange("p (h c) -> p h c", h=NSA_H)
                        dve.scalar_tensor_tensor(out=pc[:, qt, :, :], in0=s_, scalar=P ** -0.5,
                                                 in1=bcast(cmask[:, 1, qt, :], 1, NSA_H), op0=ALU.mult, op1=ALU.add)\
                           .then_inc(sem("pc_sc"), 1)
                    dve.wait_ge(sem("pc_sc"), 2)
                    dve.tensor_reduce(st[0], w_, AX.X, ALU.max).then_inc(sem("pc_max"), 1)
                    dve.wait_ge(sem("pc_max"), 1)
                    dve.tensor_tensor(w_, w_, wide(st[0]), ALU.subtract).then_inc(sem("pc_sub"), 1)
                if u == 15:
                    dve.wait_ge(sem("pc_exp"), 1)
                    for qt in range(NT):
                        dve.tensor_tensor(pc[:, qt, :, :], pc[:, qt, :, :], bcast(cmask[:, 0, qt, :], 1, NSA_H), ALU.mult)\
                           .then_inc(sem("pc_mask"), 1)
                    dve.wait_ge(sem("pc_mask"), 2)
                    dve.tensor_reduce(st[1], w_, AX.X, ALU.add).then_inc(sem("pc_st"), 1)
                    dve.wait_ge(sem("pc_st"), 1)
                    dve.tensor_scalar(st[1], st[1], TINY, None, ALU.max).then_inc(sem("pc_st"), 1)
                    dve.wait_ge(sem("pc_st"), 2)
                    dve.reciprocal(st[2], st[1]).then_inc(sem("pc_st"), 1)
                    dve.wait_ge(sem("pc_st"), 3)
                    dve.wait_ge(sem("gate"), NT)
                    dve.tensor_tensor(pcs[:, 3, :, :], pcs[:, 2, :, :], gate[:, :, 0:NGATE:3], ALU.mult)\
                       .then_inc(sem("pc_st"), 1)
                    dve.wait_ge(sem("pc_st"), 4)
                    dve.tensor_tensor(w_, w_, wide(st[3]), ALU.mult).then_inc(sem("pc"), 1)

            dve.wait_ge(sem("bias_in"), 16)
            dve.wait_ge(sem("nlam"), 1)
            dve.wait_ge(sem("blk_lo"), 2)

            def soft(u):
                h, qt, nk = unit(u)
                dve.wait_ge(sem("m1_sc"), u + 1)
                if u >= 2:
                    dve.wait_ge(sem("m1_e"), 2 * u - 2)
                b = bias[:, h + (0 if u < 16 else DIFF_H), S - nk:S]
                dve.scalar_tensor_tensor(out=scb[u % 2][:, :, 0:nk],
                                         in0=acc[u % 2][:, :, 0:nk] if u < 16 else
                                         acc[u % 2][:, 0, 0:2 * nk].rearrange("p (m k) -> p m k", m=2),
                                         scalar=(64 if u < 16 else P) ** -0.5, in1=bcast(b, 1, 2),
                                         op0=ALU.mult, op1=ALU.add).then_inc(sem("m1_sb"), 1)
                dve.wait_ge(sem("m1_sb"), u + 1)
                dve.tensor_reduce(nmx[:, u, :], scb[u % 2][:, :, 0:nk], AX.X, ALU.max, negate=True)\
                   .then_inc(sem("m1_max"), 1)

            def weights(u):
                h, qt, nk = unit(u)
                p = prb[u % 2]
                dve.wait_ge(sem("m1_e"), 2 * u + 2)
                dve.reciprocal(cof[:, u, :], psm[:, u, :]).then_inc(sem("m1_rc"), 1)
                dve.wait_ge(sem("m1_rc"), u + 1)
                if u < 16:
                    dve.tensor_tensor(cof[:, u, 1:2], cof[:, u, 1:2], lamv[:, 4:5], ALU.mult).then_inc(sem("m1_cf"), 1)
                    dve.tensor_scalar(p[:, 0, 0:nk], p[:, 0, 0:nk], cof[:, u, 0:1], None, ALU.mult)\
                       .then_inc(sem("m1_cf"), 1)
                    dve.wait_ge(sem("m1_cf"), 2 * u + 2)
                    dve.scalar_tensor_tensor(out=p[:, 0, 0:nk], in0=p[:, 1, 0:nk], scalar=cof[:, u, 1:2],
                                             in1=p[:, 0, 0:nk], op0=ALU.mult, op1=ALU.add).then_inc(sem("m1_p"), 1)
                else:
                    dve.tensor_tensor(cof[:, u, :], cof[:, u, :], gate[:, qt, 3 * h + 1:3 * h + 3], ALU.mult)\
                       .then_inc(sem("m1_cg"), 1)
                    dve.wait_ge(sem("m1_cg"), u - 15)
                    dve.tensor_scalar(p[:, 0, 0:nk], p[:, 0, 0:nk], cof[:, u, 0:1], None, ALU.mult)
                    dve.tensor_scalar(p[:, 1, 0:nk], p[:, 1, 0:nk], cof[:, u, 1:2], None, ALU.mult)\
                       .then_inc(sem("m1_p"), 1)

            soft(0)
            soft(1)
            for u in range(UNITS):
                weights(u)
                if u < CMP_CH - 1:
                    s_lo(dve, CA, 0, 0, 2 * u + 2)
                if u + 2 < UNITS:
                    soft(u + 2)
                if u < CMP_CH - 1:
                    s_lo(dve, CA, 0, 0, 2 * u + 3)
                compress(u)
                if u == 17:
                    dve.wait_ge(sem("m1_o"), 16)
                    dve.tensor_scalar(dsq[:, :, :], dsq[:, :, :], 1.0 / P, EPS, ALU.mult, ALU.add)\
                       .then_inc(sem("d_ms"), 1)
                if u == 20:
                    dve.wait_ge(sem("d_root"), 1)
                    dve.reciprocal(drs[:, :, :], drs[:, :, :]).then_inc(sem("d_rs"), 1)
                    dve.wait_ge(sem("d_rs"), 1)
                    for t in range(NT):
                        o = mix1[:, t, 0:DIFF_H * P].rearrange("p (h c) -> p h c", h=DIFF_H)
                        dve.tensor_tensor(o, o, bcast(drs[:, t, :], 2, P), ALU.mult).then_inc(sem("d_n"), 1)
                if u in (22, 24):
                    t = (u - 22) // 2
                    o = mix1[:, t, 0:DIFF_H * P].rearrange("p (h c) -> p h c", h=DIFF_H)
                    dve.wait_ge(sem("d_n"), 2)
                    dve.tensor_tensor(o, o, bcast(sub[:, :], 1, DIFF_H), ALU.mult).then_inc(sem("m1_diff"), 1)

        def mix1_ready(pe, q):
            if q == 0:
                pe.wait_ge(sem("m1_diff"), 2)
                pe.wait_ge(sem("m1_o"), UNITS)

        H2 = "in2"

        def m2_load(sp):
            w = T["hgrn_w_in_2"][0]
            with sp.Fori(0, HJ) as i:
                for c in range(HCH):
                    s_load(sp, H2, i, HCH, c, w_tile(w, CK * (c % CPG), i * GC + c // CPG * D))

        def small(level):
            b = tp[1][:, :, :].rearrange("p k t -> p (k t)")
            return b[:, level % 2 * GC:(level % 2 + 1) * GC] if level < N_STEP - 1 else b

        QUPS = 2 * (N_LEV - 1)
        KUPS = 2 + QUPS

        def halves(a, h):
            v = a[:, :, :].rearrange("p q (n two h) -> p (q n) two h", two=2, h=h)
            return v[:, :, 0, :], v[:, :, 1, :]

        def over(a, h):
            b = [list(d) for d in a.ap]
            return bass.AP(tensor=a.tensor, offset=a.offset, ap=b[:-1] + [[0, h]])

        def m2_pe(pe):
            def turn(i, j):
                pe.wait_ge(group_free, gb[H2] + j + 1 + i * HGRP)
                if j:
                    pe.wait_ge(sem("m2_t_read"), i * 3 + j)
                for k in range(HPG):
                    for t in range(NT):
                        mm = pe.transpose(tp[0][:, k, t * P:(t + 1) * P], stg[:, j, t, k * P:(k + 1) * P], ident[:, :])
                mm.then_inc(sem("m2_turned"), 1)

            def step(i, s):
                pe.wait_ge(sem("m2_kdec"), i * N_STEP + s + 1)
                if s:
                    pe.wait_ge(sem("m2_dec"), i * N_LEV + s)
                if s == N_STEP - 1:
                    pe.wait_ge(sem("m2_lev0"), i * 4 + 4)
                    pe.wait_ge(sem("m2_lev1"), i * 4 + 4)
                elif s >= 2:
                    pe.wait_ge(sem(f"m2_lev{s % 2}"), i * 4 + s // 2)
                q, k = (qT if s == 0 else qd[s % 2]), kd[s % 2]
                if s < 7:
                    for hd in range(HPG):
                        for t in range(NT):
                            for j in range(4):
                                jt = j ^ 1 if s == 6 else j
                                c = (hd * NT + t) * 32
                                mm = pe.matmul(small(s)[32 * j:32 * j + 32, c:c + 32],
                                               k[:, hd, t * P + 32 * j:t * P + 32 * j + 32],
                                               q[:, hd, t * P + 32 * jt:t * P + 32 * jt + 32], start=True, stop=True)
                elif s == 7:
                    for hd in range(HPG):
                        for t in range(NT):
                            for a in range(2):
                                c = (hd * NT + t) * 64
                                mm = pe.matmul(small(s)[64 * a:64 * a + 64, c:c + 64],
                                               k[:, hd, t * P + 64 * a:t * P + 64 * a + 64],
                                               q[:, hd, t * P + 64 * (1 - a):t * P + 64 * (2 - a)],
                                               start=True, stop=True)
                else:
                    for hd in range(HPG):
                        for t in range(NT):
                            c = (hd * NT + t) * P
                            mm = pe.matmul(small(s)[:, c:c + P], k[:, hd, t * P:(t + 1) * P],
                                           q[:, hd, (1 - t) * P:(2 - t) * P], start=True, stop=True)
                mm.then_inc(sem("m2_step"), 1)

            def outs(i):
                pe.wait_ge(sem("m2_at"), i + 1)
                o = small(N_STEP - 1)
                for t in range(NT):
                    for hd in range(HPG):
                        c = (t * HPG + hd) * P
                        for s in range(NT):
                            mm = pe.matmul(o[:, c:c + P], at[:, hd, s, t * P:(t + 1) * P],
                                           vt[:, s, hd * P:(hd + 1) * P], start=(s == 0), stop=(s == NT - 1))
                mm.then_inc(sem("m2_pv"), 1)

            def body(i, first):
                for c in range(HCH):
                    if c == 0:
                        pe.wait_ge(group_free, gb[H2] + i * HGRP)
                    elif c % CPG == 0:
                        group(pe, gb[H2] + c // CPG + i * HGRP)
                    if first:
                        lead_pe(pe, H2, c, x, x_ready("down1"))
                    products(pe, cb[H2] + c + i * HCH, c % RING, acc[c // CPG % 2], ahi, alo, CK * (c % CPG), KT,
                             "in2" if first and c < CPG else None)
                    if c in (10, 18, 26):
                        turn(i, c // CPG - 1)
                    if c == 31:
                        step(i, 0)
                    if c in (31, 33, 35, 37, 39):
                        step(i, 1 + (c - 31) // 2)
                    if not first and c in (1, 3, 5):
                        step(i - 1, 6 + c // 2)
                    if not first and c == 11:
                        outs(i - 1)
            body(0, True)
            with pe.Fori(1, HJ) as i:
                body(i, False)
            for s in range(6, N_STEP):
                step(HJ - 1, s)
            outs(HJ - 1)

        def m2_act(act):
            def full(i, g):
                act.wait_ge(chunk_used, cb[H2] + CPG * (g + 1) + i * HCH)

            def evacuate(i, g):
                full(i, g)
                for t in range(NT):
                    dst = gs[:, t, :] if g == 4 else vt[:, t, :] if g == 3 else stg[:, g, t, :]
                    m = act.activation(dst, acc[g % 2][:, t, :],
                                       (ACT.Silu, ACT.Sigmoid, ACT.Sigmoid, ACT.Copy, ACT.Silu)[g],
                                       scale=rstd[:, 2, t:t + 1])
                m.then_inc(group_free, 1)

            def turned(i, j, first):
                act.wait_ge(sem("m2_turned"), i * 3 + (j + 1))
                if j == 0 and not first:
                    act.wait_ge(sem("m2_dec"), i * N_LEV)
                if j:
                    act.activation((kf, kb)[j - 1][:, :, :], tp[0][:, :, :], ACT.Identity, bias=1.0, scale=-1.0)
                act.activation((qT, pf, ib)[j][:, :, :], tp[0][:, :, :], ACT.Copy).then_inc(sem("m2_t_read"), 1)

            def level(i, s):
                act.wait_ge(sem("m2_step"), i * N_STEP + s + 1)
                if s == 6:
                    for j in range(4):
                        r = slice(32 * j, 32 * j + 32)
                        m = act.activation(strided(at[r, 0, 0, 32 * (j ^ 1):32 * (j ^ 1) + 1], [[NT * S, HPG], [S + P, NT], [1, 32]]),
                                           small(6)[r, 0:HPG * NT * 32].rearrange("p (a b c) -> p a b c", a=HPG, b=NT),
                                           ACT.Copy)
                    m.then_inc(sem("m2_lev0"), 1)
                elif s == 7:
                    for a in range(2):
                        r = slice(64 * a, 64 * a + 64)
                        m = act.activation(strided(at[r, 0, 0, 64 * (1 - a):64 * (1 - a) + 1], [[NT * S, HPG], [S + P, NT], [1, 64]]),
                                           small(7)[r, 0:HPG * NT * 64].rearrange("p (a b c) -> p a b c", a=HPG, b=NT),
                                           ACT.Copy)
                    m.then_inc(sem("m2_lev1"), 1)
                else:
                    act.activation(strided(at[:, 0, 0, P:P + 1], [[NT * S, HPG], [P, NT], [1, P]]),
                                   small(8).rearrange("p (a b c) -> p a b c", a=HPG, b=NT), ACT.Copy)\
                       .then_inc(sem("m2_at"), 1)

            def diagonal(i):
                act.wait_ge(sem("m2_lev1"), i * 4 + 3)
                for j in range(4):
                    r = slice(32 * j, 32 * j + 32)
                    act.activation(strided(at[r, 0, 0, 32 * j:32 * j + 1], [[NT * S, HPG], [S + P, NT], [1, 32]]),
                                   ad[r, :, :, :], ACT.Copy)

            def squares(i):
                act.wait_ge(sem("m2_pv"), i + 1)
                act.activation(sgm[:, :, :].rearrange("p n c -> p (n c)"), small(N_STEP - 1), ACT.Square)\
                   .then_inc(sem("m2_sq"), 1)

            def tail(i, c):
                if c == 3:
                    evacuate(i, 4)
                if c in (3, 6, 9):
                    level(i, 5 + c // 3)
                if c == 7:
                    diagonal(i)
                if c == 14:
                    squares(i)

            def body(i, first):
                for c in range(LEAD if first else 0, HCH):
                    if first:
                        lead_act(act, H2, c, 2)
                    s_hi(act, H2, i, HCH, c)
                    if c == 7 and first:
                        sumsq_act(act, "in2", 2, sem("down1_x"), 8)
                        act.wait_ge(sem("in2_rstd"), 1)
                    if not first:
                        tail(i - 1, c)
                    if c in (11, 19, 27, 35):
                        evacuate(i, (c - 11) // 8)
                    if c in (12, 20, 28):
                        turned(i, (c - 12) // 8, first)
            body(0, True)
            with act.Fori(1, HJ) as i:
                body(i, False)
            for c in range(LEAD):
                s_hi(act, "out2", 0, 0, c)
            for c in range(18):
                tail(HJ - 1, c)
            act.wait_ge(sem("h_ms"), 1)
            act.activation(hrs[:, :, :], hsq[:, :, :], ACT.Sqrt).then_inc(sem("h_root"), 1)

        def m2_dve(dve):
            def decay(i, s):
                if s >= 2:
                    h = 2 ** (s - 2)
                    (pf1, pf2), (ib1, ib2) = halves(pf, h), halves(ib, h)
                    dve.wait_ge(sem("m2_kup"), i * KUPS + 2 * s)
                    dve.tensor_tensor(pf2, pf2, over(pf1[:, :, h - 1:h], h), ALU.mult).then_inc(sem("m2_up"), 1)
                    dve.tensor_tensor(ib1, ib1, over(ib2[:, :, 0:1], h), ALU.mult).then_inc(sem("m2_up"), 1)
                    dve.wait_ge(sem("m2_up"), i * QUPS + 2 * (s - 1))
                    dve.wait_ge(sem("m2_step"), i * N_STEP + s - 1)
                else:
                    dve.wait_ge(sem("m2_t_read"), i * 3 + 3)
                h = 2 ** (s - 1)
                (q1, q2), (_, pf2), (ib1, _) = halves(qT, h), halves(pf, h), halves(ib, h)
                qd1, qd2 = halves(qd[s % 2], h)
                dve.tensor_tensor(qd2, q2, pf2, ALU.mult)
                dve.tensor_tensor(qd1, q1, ib1, ALU.mult).then_inc(sem("m2_dec"), 1)

            def level(i, s):
                dve.wait_ge(sem("m2_step"), i * N_STEP + s + 1)
                if s == 0:
                    dve.tensor_tensor(ad[:, :, :, :].rearrange("p a b c -> p (a b) c"),
                                      small(0)[:, 0:HPG * NT * 32].rearrange("p (a c) -> p a c", c=32),
                                      bcast(lmask[:, 5, :], 1, HPG * NT), ALU.mult).then_inc(sem("m2_lev0"), 1)
                    return
                else:
                    dve.wait_ge(sem(f"m2_lev{(s - 1) % 2}"), i * 4 + (s - 1) // 2 + 1)
                dve.tensor_tensor(lpick[:, :, :], small(s)[:, 0:HPG * NT * 32].rearrange("p (a c) -> p a c", c=32),
                                  bcast(lmask[:, s - 1, :], 1, HPG * NT), ALU.mult).then_inc(sem("m2_pick"), 1)
                dve.wait_ge(sem("m2_pick"), i * 5 + s)
                a = ad[:, :, :, :].rearrange("p a b c -> p (a b) c")
                dve.tensor_tensor(a, a, lpick[:, :, :], ALU.add).then_inc(sem(f"m2_lev{s % 2}"), 1)

            def outputs(i):
                dve.wait_ge(sem("m2_pv"), i + 1)
                o = small(N_STEP - 1).rearrange("p (n c) -> p n c", n=NT)
                dve.wait_ge(sem("m2_sq"), i + 1)
                dve.tensor_tensor(mix2[:, :, bass.ds(i * GC, GC)], o, gs[:, :, :], ALU.mult)
                dve.tensor_reduce(hsq[:, :, bass.ds(i * HPG, HPG)],
                                  sgm[:, :, :].rearrange("p n (h c) -> p n h c", c=P), AX.X, ALU.add)\
                   .then_inc(sem("m2_o"), 1)

            def tail(i, c):
                if c in (1, 3):
                    decay(i, 7 + c // 2)
                if c in (0, 2):
                    level(i, 4 + c // 2)
                if c == 14:
                    dve.wait_ge(sem("m2_gs"), i + 1)
                    outputs(i)

            def body(i, first):
                for c in range(LEAD if first else 0, HCH):
                    if first:
                        lead_dve(dve, H2, c, 2, add_rows(dve, "down1", 1))
                    s_lo(dve, H2, i, HCH, c)
                    if c == 7 and first:
                        sumsq_dve(dve, "in2", 2)
                        dve.wait_ge(sem("m2_gn"), 32)
                    if not first:
                        tail(i - 1, c)
                    if c in (29, 31, 33, 35, 37, 39):
                        decay(i, 1 + (c - 29) // 2)
                    if c in (33, 34, 36, 38):
                        level(i, (33, 34, 36, 38).index(c))
            body(0, True)
            with dve.Fori(1, HJ) as i:
                body(i, False)
            for c in range(LEAD):
                s_lo(dve, "out2", 0, 0, c)
            for c in range(18):
                tail(HJ - 1, c)
            dve.wait_ge(sem("m2_o"), HJ)
            dve.tensor_scalar(hsq[:, :, :], hsq[:, :, :], 1.0 / P, EPS, ALU.mult, ALU.add).then_inc(sem("h_ms"), 1)
            dve.wait_ge(sem("h_root"), 1)
            dve.reciprocal(hrs[:, :, :], hrs[:, :, :]).then_inc(sem("h_rs"), 1)
            dve.wait_ge(sem("h_rs"), 1)

        def m2_pool(pool):
            def keys(i, s):
                if s == 0:
                    pool.wait_ge(sem("m2_t_read"), i * 3 + 3)
                    pool.tensor_tensor(kd[0][:, :, :], kf[:, :, :], kb[:, :, :], ALU.add).then_inc(sem("m2_kdec"), 1)
                    return
                h = 2 ** (s - 1)
                (kf1, _), (_, kb2), (sf1, sf2), (eb1, eb2) = halves(kf, h), halves(kb, h), halves(sf, h), halves(eb, h)
                kd1, kd2 = halves(kd[s % 2], h)
                up = sem("m2_kup")
                if s == 1:
                    pool.tensor_copy(kd1, kf1)
                    pool.tensor_copy(kd2, kb2).then_inc(sem("m2_kdec"), 1)
                    pool.memset(sf2, 1.0).then_inc(up, 1)
                    pool.memset(eb1, 1.0).then_inc(up, 1)
                    pool.tensor_copy(sf1, halves(pf, h)[1]).then_inc(up, 1)
                    pool.tensor_copy(eb2, halves(ib, h)[0]).then_inc(up, 1)
                    return
                pool.wait_ge(sem("m2_step"), i * N_STEP + s - 1)
                pool.wait_ge(up, i * KUPS + 2 * s)
                pool.tensor_tensor(kd1, kf1, sf1, ALU.mult)
                pool.tensor_tensor(kd2, kb2, eb2, ALU.mult).then_inc(sem("m2_kdec"), 1)
                if s < N_LEV:
                    pool.wait_ge(sem("m2_up"), i * QUPS + 2 * (s - 1))
                    pool.tensor_tensor(sf1, sf1, over(halves(pf, h)[1][:, :, h - 1:h], h), ALU.mult).then_inc(up, 1)
                    pool.tensor_tensor(eb2, eb2, over(halves(ib, h)[0][:, :, 0:1], h), ALU.mult).then_inc(up, 1)

            pool.wait_ge(sem("m2_gn"), 32)
            with pool.Fori(0, HJ) as i:
                for s in range(N_STEP):
                    keys(i, s)
                pool.wait_ge(group_free, gb[H2] + HGRP + i * HGRP)
                g4 = gs[:, :, :].rearrange("p n (h c) -> p (n h) c", c=P)
                pool.tensor_tensor(g4, g4, bcast(gnb[:, :], 1, NT * HPG), ALU.mult).then_inc(sem("m2_gs"), 1)

        def norm_heads(dve):
            def norm(q):
                for t in range(NT):
                    o = mix2[:, t, q * GC:(q + 1) * GC].rearrange("p (h c) -> p h c", c=P)
                    dve.tensor_tensor(o, o, bcast(hrs[:, t, q * HPG:(q + 1) * HPG], 2, P), ALU.mult)\
                       .then_inc(sem("m2_mix"), 1)
            return norm

        def mix2_ready(pe, q):
            pe.wait_ge(sem("m2_mix"), 2 * q + 2)

        def x0_ready(pe, q):
            pe.wait_ge(sem(f"x_in{q}"), 16)

        def gain_load(pool, ph, dst, name):
            pool.dma_start(dst[:, :], bcast(T[name][0], 0, P)).then_inc(sem(f"{ph}_gain"), 16)

        block = ctx.enter_context(nc.Block())

        @block.sync
        def _(sp):
            rows_load(sp, ROWS[0::2])
            x_load(sp, (0, 1))
            in1_load(sp)
            m1_load(sp)
            back_load(sp, "out1", T["w_out"][0], CPG)
            up_load(sp, "up1", T["w_up"][0])
            back_load(sp, "down1", T["w_down"][0], DCH)
            m2_load(sp)
            back_load(sp, "out2", T["hgrn_w_out_2"][0], CPG)
            up_load(sp, "up2", T["ffn_w_in_2"][0])
            back_load(sp, "down2", T["ffn_w_out_2"][0], DCH)
            for q in range(4):
                c = slice(q * GC, (q + 1) * GC)
                sp.wait_ge(sem("down2_x"), 2 * q + 2)
                sp.dma_start(T["out"][0][:, c].rearrange("(n p) c -> p n c", p=P), x[:, :, c]).then_inc(sem("out"), 16)
            sp.wait_ge(sem("out"), 64)

        @block.gpsimd
        def _(pool):
            setup_pool(pool)
            pool.wait_ge(sem("m1_o"), UNITS)
            gain_load(pool, "out1", gbo1, "post_mix_norm")
            up_pool(pool, "up1")
            pool.wait_ge(chunk_used, cb["down1"])
            gain_load(pool, "down1", gbd, "post_ffn_norm")
            pool.wait_ge(chunk_used, cb["in2"])
            pool.dma_start(gnb[:, :], bcast(T["hgrn_gnorm_2"][0], 0, P)).then_inc(sem("m2_gn"), 16)
            pool.dma_start(lmask[:, :, :], T["lmask"]).then_inc(sem("m2_gn"), 16)
            gain_load(pool, "out2", gbo2, "norm_post_mix_2")
            m2_pool(pool)
            up_pool(pool, "up2")
            pool.wait_ge(chunk_used, cb["down2"])
            gain_load(pool, "down2", gbd, "norm_post_ffn_2")

        @block.tensor
        def _(pe):
            setup_pe(pe)
            in1_pe(pe)
            m1_pe(pe)
            back_pe(pe, "out1", ahi, alo, CPG, src=mix1, src_ready=mix1_ready)
            up_pe(pe, "up1", x_ready("out1"))
            back_pe(pe, "down1", hhi, hlo, DCH, sem("up1_hid"), FG, FG + 1)
            m2_pe(pe)
            back_pe(pe, "out2", ahi, alo, CPG, src=mix2, src_ready=mix2_ready)
            up_pe(pe, "up2", x_ready("out2"))
            back_pe(pe, "down2", hhi, hlo, DCH, sem("up2_hid"), FG, FG + 1)

        @block.scalar
        def _(act):
            rows_load(act, ROWS[1::2])
            in1_act(act)
            m1_act(act)
            back_act(act, "out1", 0, CPG, first_too=True)
            up_act(act, "up1", 0, sem("out1_x"), 8)
            back_act(act, "down1", 1, DCH)
            m2_act(act)
            back_act(act, "out2", 2, CPG, first_too=True)
            up_act(act, "up2", 1, sem("out2_x"), 8)
            back_act(act, "down2", 3, DCH, last=True)

        @block.vector
        def _(dve):
            setup_dve(dve)
            in1_dve(dve)
            m1_dve(dve)
            back_dve(dve, "out1", 0, CPG, gbo1, source=lambda q: None)
            up_dve(dve, "up1", 0, add_rows(dve, "out1", 0))
            back_dve(dve, "down1", 1, DCH, gbd)
            m2_dve(dve)
            back_dve(dve, "out2", 2, CPG, gbo2, source=norm_heads(dve))
            up_dve(dve, "up2", 1, add_rows(dve, "out2", 2))
            back_dve(dve, "down2", 3, DCH, gbd, last=True)
            for q in range(4):
                add_rows(dve, "down2", 3)(q)


_INS = ["x", "pre_mix_norm", "w_in", "lambda_q1", "lambda_k1", "lambda_q2", "lambda_k2", "diff_subln", "cmp_pos_k",
        "cmp_pos_v", "cmp_k_w1", "cmp_k_w2", "cmp_v_w1", "cmp_v_w2", "rel_bias", "w_out", "post_mix_norm",
        "pre_ffn_norm", "w_up", "conv_w", "conv_b", "w_down", "post_ffn_norm", "hgrn_w_in_2", "hgrn_w_out_2",
        "hgrn_gnorm_2", "ffn_w_in_2", "ffn_w_conv_2", "ffn_w_out_2", "norm_pre_mix_2", "norm_post_mix_2",
        "norm_pre_ffn_2", "norm_post_ffn_2"]


def _constants():
    import numpy as np
    delta = S - 1 - np.arange(TOEP)
    n = np.maximum(delta, 0)
    exact = N_BUCKETS // 2
    large = exact + (np.log(np.maximum(n, 1) / exact) / math.log(128 / exact) * (N_BUCKETS - exact)).astype(np.int32)
    bucket = np.where(n < exact, n, np.minimum(large, N_BUCKETS - 1))
    row = np.where(delta < 0, N_BUCKETS, bucket)
    onehot = (np.arange(N_BUCKETS + 1)[:, None] == row[None, :]).astype(np.float32)
    tok = np.arange(NT)[None, :, None] * P + np.arange(P)[:, None, None]
    seen = (np.arange(NC_)[None, None, :] * CMP_STRIDE + CMP_L - 1 <= tok).astype(np.float32)
    cmask = np.stack([seen, (1 - seen) * np.float32(NEG)], axis=1).astype(np.float32)
    s_ = (np.arange(P) % 32)[:, None, None]
    t_ = np.arange(32)[None, None, :]
    h = 2 ** np.arange(5)[None, :, None]
    m = (s_ // (2 * h) == t_ // (2 * h)) & (s_ // h != t_ // h)
    lmask = np.concatenate([m, s_ == t_], axis=1).astype(np.float32)
    return {"onehot": onehot, "cmask": np.ascontiguousarray(cmask), "lmask": np.ascontiguousarray(lmask)}


def kernel(**inputs):
    import numpy as _np
    import concourse.bacc as _bacc
    from concourse.bass_utils import run_bass_kernel_spmd as _run

    nc = _bacc.Bacc("TRN2", target_bir_lowering=False, num_devices=1)
    arrays, args = {}, {}
    for name in _INS:
        a = _np.ascontiguousarray(inputs[name])
        arrays[f"in_{name}_dram"] = a
        args[name] = nc.dram_tensor(f"in_{name}_dram", a.shape, mybir.dt.from_np(a.dtype), kind="ExternalInput").ap()
    for name, a in _constants().items():
        arrays[f"const_{name}_dram"] = a
        args[name] = nc.dram_tensor(f"const_{name}_dram", a.shape, mybir.dt.from_np(a.dtype), kind="ExternalInput").ap()
    args["scratch"] = nc.dram_tensor("scratch_dram", (16, P, TOEP), F32).ap()
    args["out"] = nc.dram_tensor("out_0_dram", (1, S, D), F32, kind="ExternalOutput").ap()
    bass_two_blocks(nc, args)
    r = _run(nc, [arrays], core_ids=[0])
    return r.results[0]["out_0_dram"]
```
